# Optimizing a Trainium2 kernel written in Bass

```python
import jax, jax.numpy as jnp
from jax import lax
import numpy as np
import math

D_MODEL = 1024
BATCH = 1
SEQ = 256
DEPTH = 2

CTX_LEN = 256
GRID_W = 64
N_MOD = 9
D_FF = 2816
NORM_EPS = 1e-6
RWKV_HEAD = 64
D_RWKV = 3 * D_MODEL // 4
RWKV_HEADS = D_RWKV // RWKV_HEAD
DECAY_RANK = 64
ICLR_RANK = 64
GATE_RANK = 128
DECAY_SCALE = 0.606531
GN_EPS = 64e-5
D_FOURIER = D_MODEL // 4
FOURIER_GROUPS = 4
FOURIER_GROUP = D_FOURIER // FOURIER_GROUPS
D_A_IN = 3 * D_RWKV + DECAY_RANK + ICLR_RANK + GATE_RANK
D_EVEN_IN = D_A_IN + D_FOURIER
D_MIX_EVEN = D_RWKV + D_FOURIER
D_CONV = 3 * D_MODEL // 4
CONV_WIDTH = 31
POOL_WIDTHS = (2, 4, 8, 16)
D_POOL = D_MODEL // 4
POOL_GROUP = D_POOL // len(POOL_WIDTHS)
D_ODD_IN = 2 * D_CONV + D_POOL
D_MIX_ODD = D_CONV + D_POOL


def rmsnorm(x, g):
    xf = x.astype(jnp.float32)
    y = xf * lax.rsqrt(jnp.mean(xf * xf, axis=-1, keepdims=True) + NORM_EPS)
    return y.astype(x.dtype) * g

def modulate(h, g, shift, scale):
    return rmsnorm(h, g) * (1 + scale) + shift

def swiglu(y, w_gu, w_down):
    gate, up = jnp.split(y @ w_gu, 2, axis=-1)
    return (jax.nn.silu(gate) * up) @ w_down

def half_ffn(h, m, off, g, w_gu, w_down):
    y = modulate(h, g, m[off], m[off + 1])
    return h + 0.5 * m[off + 2] * swiglu(y, w_gu, w_down)

def to_column_major(u):
    b, n = u.shape[0], u.shape[1]
    rows = n // GRID_W
    return u.reshape(b, rows, GRID_W, -1).transpose(0, 2, 1, 3).reshape(b, n, -1)

def from_column_major(u):
    b, n = u.shape[0], u.shape[1]
    rows = n // GRID_W
    return u.reshape(b, GRID_W, rows, -1).transpose(0, 2, 1, 3).reshape(b, n, -1)

def token_shift(z, mu):
    zp = jnp.pad(z, ((0, 0), (1, 1), (0, 0)))
    return z + mu * (0.5 * (zp[:, :-2] + zp[:, 2:]) - z)

def fourier_mix(u):
    b, n, _ = u.shape
    uf = u.astype(jnp.float32).reshape(b, n, FOURIER_GROUPS, FOURIER_GROUP)
    out = jnp.fft.fft2(uf, axes=(1, 3), norm='ortho').real
    return out.reshape(b, n, D_FOURIER).astype(u.dtype)

def rwkv_features(zA, w0, w_up, a0, a_up, g_up, k_k, k_a):
    b, n, _ = zA.shape
    heads = lambda u: u.reshape(b, n, RWKV_HEADS, RWKV_HEAD)
    s = [D_RWKV, 2 * D_RWKV, 3 * D_RWKV, 3 * D_RWKV + DECAY_RANK, 3 * D_RWKV + DECAY_RANK + ICLR_RANK]
    r, k, v, wd, ad, gd = jnp.split(zA, s, axis=-1)
    g = jax.nn.sigmoid(gd) @ g_up
    kk = heads(k * k_k).astype(jnp.float32)
    kk = kk / jnp.maximum(jnp.sqrt(jnp.sum(kk * kk, axis=-1, keepdims=True)), 1e-12)
    dirs = []
    for d in range(2):
        w = jnp.exp(-DECAY_SCALE * jax.nn.sigmoid(w0[d] + jnp.tanh(wd) @ w_up[d]))
        a = jax.nn.sigmoid(a0[d] + ad @ a_up[d])
        kd = k * (1 + (a - 1) * k_a)
        dirs.append((heads(w), heads(kd), kk * heads(a).astype(jnp.float32)))
    return heads(r), heads(v), kk, g, dirs

def wkv_scan(S0, r, w, k, v, kk, bb, reverse):
    tm = lambda u: jnp.moveaxis(u.astype(jnp.float32), 1, 0)
    xs = (tm(r), tm(w), tm(k), tm(v), tm(kk), tm(bb))

    def step(S, inp):
        rt, wt, kt, vt, kkt, bt = inp
        sk = jnp.einsum('bhij,bhj->bhi', S, kkt)
        S = S * wt[:, :, None, :] - sk[..., None] * bt[:, :, None, :] + vt[..., None] * kt[:, :, None, :]
        return S, jnp.einsum('bhij,bhj->bhi', S, rt)

    S, ys = lax.scan(step, S0, xs, reverse=reverse)
    return S, jnp.moveaxis(ys, 0, 1)

def rwkv_output(y, r, kds, v, g, r_k, gn_w, gn_b):
    b, n = y.shape[0], y.shape[1]
    mu = jnp.mean(y, axis=-1, keepdims=True)
    var = jnp.mean(jnp.square(y - mu), axis=-1, keepdims=True)
    yn = ((y - mu) * lax.rsqrt(var + GN_EPS)).reshape(b, n, D_RWKV) * gn_w + gn_b
    rk = r_k.reshape(RWKV_HEADS, RWKV_HEAD)
    coef = jnp.sum(r * kds[0] * rk, axis=-1, keepdims=True) + jnp.sum(r * kds[1] * rk, axis=-1, keepdims=True)
    bonus = (coef * v).reshape(b, n, D_RWKV)
    return (yn.astype(g.dtype) + bonus) * g

def even_mixer(y_ctx, y_lat, col_major, w_in, mu, w0, w_up, a0, a_up, g_up, k_k, k_a, r_k, gn_w, gn_b, w_out):
    z_ctx = y_ctx @ w_in
    z_lat = y_lat @ w_in
    f_ctx = fourier_mix(z_ctx[..., D_A_IN:])
    f_lat = fourier_mix(z_lat[..., D_A_IN:])
    zA_ctx = z_ctx[..., :D_A_IN]
    zA_lat = z_lat[..., :D_A_IN]
    if col_major:
        zA_lat = to_column_major(zA_lat)
    zA_ctx = token_shift(zA_ctx, mu)
    zA_lat = token_shift(zA_lat, mu)
    fargs = (w0, w_up, a0, a_up, g_up, k_k, k_a)
    r_c, v_c, kk_c, g_c, dirs_c = rwkv_features(zA_ctx, *fargs)
    r_l, v_l, kk_l, g_l, dirs_l = rwkv_features(zA_lat, *fargs)
    S0 = jnp.zeros((y_ctx.shape[0], RWKV_HEADS, RWKV_HEAD, RWKV_HEAD), jnp.float32)
    ys_c, ys_l = [], []
    for d in range(2):
        w_c, kd_c, b_c = dirs_c[d]
        w_l, kd_l, b_l = dirs_l[d]
        S_c, yc = wkv_scan(S0, r_c, w_c, kd_c, v_c, kk_c, b_c, reverse=(d == 1))
        _, yl = wkv_scan(S_c, r_l, w_l, kd_l, v_l, kk_l, b_l, reverse=(d == 1))
        ys_c.append(yc)
        ys_l.append(yl)
    o_ctx = rwkv_output(ys_c[0] + ys_c[1], r_c, (dirs_c[0][1], dirs_c[1][1]), v_c, g_c, r_k, gn_w, gn_b)
    o_lat = rwkv_output(ys_l[0] + ys_l[1], r_l, (dirs_l[0][1], dirs_l[1][1]), v_l, g_l, r_k, gn_w, gn_b)
    if col_major:
        o_lat = from_column_major(o_lat)
    out_ctx = jnp.concatenate([o_ctx, f_ctx], axis=-1) @ w_out
    out_lat = jnp.concatenate([o_lat, f_lat], axis=-1) @ w_out
    return out_ctx, out_lat

def centered_pool_minus_self(u, width):
    n = u.shape[1]
    uf = u.astype(jnp.float32)
    cs = jnp.pad(jnp.cumsum(uf, axis=1), ((0, 0), (1, 0), (0, 0)))
    t = jnp.arange(n)
    lo = jnp.maximum(t - width // 2, 0)
    hi = jnp.minimum(t + (width - 1 - width // 2), n - 1)
    total = jnp.take(cs, hi + 1, axis=1) - jnp.take(cs, lo, axis=1)
    mean = total / (hi - lo + 1).astype(jnp.float32)[None, :, None]
    return (mean - uf).astype(u.dtype)

def odd_mixer(y, w_in, conv_w, conv_b, cnorm_g, pool_w, pool_scale, w_out):
    b, n, _ = y.shape
    z = y @ w_in
    ga, gb, q = jnp.split(z, [D_CONV, 2 * D_CONV], axis=-1)
    u = ga * jax.nn.sigmoid(gb)
    u = lax.conv_general_dilated(u, conv_w[:, None, :], window_strides=(1,),
                                 padding=[(CONV_WIDTH // 2, CONV_WIDTH // 2)],
                                 dimension_numbers=('NWC', 'WIO', 'NWC'),
                                 feature_group_count=D_CONV) + conv_b
    u = jax.nn.silu(rmsnorm(u, cnorm_g))
    qg = jnp.split(q, len(POOL_WIDTHS), axis=-1)
    p = jnp.stack([centered_pool_minus_self(qi, wd) for qi, wd in zip(qg, POOL_WIDTHS)], axis=2)
    p = jnp.einsum('bngc,gcd->bngd', p, pool_w).reshape(b, n, D_POOL) * pool_scale
    return jnp.concatenate([u, p], axis=-1) @ w_out

def first_inputs(seed: int = 0) -> dict:
    key = jax.random.key(seed)
    ks = iter(jax.random.split(key, 40))
    nrm = lambda shape, scale: scale * jax.random.normal(next(ks), shape, jnp.float32)
    ne, no = (DEPTH + 1) // 2, DEPTH // 2
    D = D_MODEL
    return {
        'x': nrm((BATCH, SEQ, D), 1.0),
        'c': nrm((BATCH, D), 1.0),
        'ctx': nrm((BATCH, CTX_LEN, D), 1.0),
        'c_ctx': nrm((D,), 1.0),
        'ada_w': nrm((DEPTH, D, N_MOD * D), 0.5 * D ** -0.5),
        'ada_b': nrm((DEPTH, N_MOD * D), 0.02),
        'norm_g': 1.0 + nrm((DEPTH, 3, D), 0.05),
        'ffn1_w_gu': nrm((DEPTH, D, 2 * D_FF), D ** -0.5),
        'ffn1_w_down': nrm((DEPTH, D_FF, D), D_FF ** -0.5),
        'ffn2_w_gu': nrm((DEPTH, D, 2 * D_FF), D ** -0.5),
        'ffn2_w_down': nrm((DEPTH, D_FF, D), D_FF ** -0.5),
        'e_w_in': nrm((ne, D, D_EVEN_IN), D ** -0.5),
        'e_mu': jax.random.uniform(next(ks), (ne, D_A_IN), jnp.float32),
        'e_w0': -1.0 + nrm((ne, 2, D_RWKV), 0.5),
        'e_w_up': nrm((ne, 2, DECAY_RANK, D_RWKV), DECAY_RANK ** -0.5),
        'e_a0': nrm((ne, 2, D_RWKV), 0.5),
        'e_a_up': nrm((ne, 2, ICLR_RANK, D_RWKV), ICLR_RANK ** -0.5),
        'e_g_up': nrm((ne, GATE_RANK, D_RWKV), GATE_RANK ** -0.5),
        'e_k_k': 1.0 + nrm((ne, D_RWKV), 0.1),
        'e_k_a': 1.0 + nrm((ne, D_RWKV), 0.1),
        'e_r_k': nrm((ne, D_RWKV), 0.1),
        'e_gn_w': 1.0 + nrm((ne, D_RWKV), 0.05),
        'e_gn_b': nrm((ne, D_RWKV), 0.02),
        'e_w_out': nrm((ne, D_MIX_EVEN, D), D_MIX_EVEN ** -0.5),
        'o_w_in': nrm((no, D, D_ODD_IN), D ** -0.5),
        'o_conv_w': nrm((no, CONV_WIDTH, D_CONV), CONV_WIDTH ** -0.5),
        'o_conv_b': nrm((no, D_CONV), 0.02),
        'o_cnorm_g': 1.0 + nrm((no, D_CONV), 0.05),
        'o_pool_w': nrm((no, len(POOL_WIDTHS), POOL_GROUP, POOL_GROUP), POOL_GROUP ** -0.5),
        'o_pool_scale': 1.0 + nrm((no, D_POOL), 0.1),
        'o_w_out': nrm((no, D_MIX_ODD, D), D_MIX_ODD ** -0.5),
        'final_g': 1.0 + nrm((D,), 0.05),
    }

def first_block(x, c, ctx, c_ctx, ada_w, ada_b, norm_g, ffn1_w_gu, ffn1_w_down, ffn2_w_gu, ffn2_w_down,
              e_w_in, e_mu, e_w0, e_w_up, e_a0, e_a_up, e_g_up, e_k_k, e_k_a, e_r_k, e_gn_w, e_gn_b, e_w_out,
              o_w_in, o_conv_w, o_conv_b, o_cnorm_g, o_pool_w, o_pool_scale, o_w_out, final_g):
    h_lat, h_ctx = x, ctx
    for i in range(DEPTH):
        j = i // 2
        with_ctx = not (i == DEPTH - 1 and i % 2 == 1)
        m_lat = jnp.split((jax.nn.silu(c) @ ada_w[i] + ada_b[i])[:, None, :], N_MOD, axis=-1)
        if with_ctx:
            m_ctx = jnp.split((jax.nn.silu(c_ctx) @ ada_w[i] + ada_b[i])[None, None, :], N_MOD, axis=-1)
            h_ctx = half_ffn(h_ctx, m_ctx, 0, norm_g[i, 0], ffn1_w_gu[i], ffn1_w_down[i])
        h_lat = half_ffn(h_lat, m_lat, 0, norm_g[i, 0], ffn1_w_gu[i], ffn1_w_down[i])
        y_lat = modulate(h_lat, norm_g[i, 1], m_lat[3], m_lat[4])
        if i % 2 == 0:
            y_ctx = modulate(h_ctx, norm_g[i, 1], m_ctx[3], m_ctx[4])
            o_ctx, o_lat = even_mixer(y_ctx, y_lat, j % 2 == 1, e_w_in[j], e_mu[j], e_w0[j], e_w_up[j],
                                      e_a0[j], e_a_up[j], e_g_up[j], e_k_k[j], e_k_a[j], e_r_k[j],
                                      e_gn_w[j], e_gn_b[j], e_w_out[j])
            h_ctx = h_ctx + m_ctx[5] * o_ctx
            h_lat = h_lat + m_lat[5] * o_lat
        else:
            odd_args = (o_w_in[j], o_conv_w[j], o_conv_b[j], o_cnorm_g[j], o_pool_w[j], o_pool_scale[j], o_w_out[j])
            h_lat = h_lat + m_lat[5] * odd_mixer(y_lat, *odd_args)
            if with_ctx:
                y_ctx = modulate(h_ctx, norm_g[i, 1], m_ctx[3], m_ctx[4])
                h_ctx = h_ctx + m_ctx[5] * odd_mixer(y_ctx, *odd_args)
        if with_ctx:
            h_ctx = half_ffn(h_ctx, m_ctx, 6, norm_g[i, 2], ffn2_w_gu[i], ffn2_w_down[i])
        h_lat = half_ffn(h_lat, m_lat, 6, norm_g[i, 2], ffn2_w_gu[i], ffn2_w_down[i])
    return rmsnorm(h_lat, final_g)


DN_ALPHA = (2.0 * DEPTH) ** 0.25
DN_BETA = (8.0 * DEPTH) ** -0.25
LN_EPS = 1e-5
RG_WIDTH = D_MODEL
RG_BLOCKS = 16
RG_BLOCK = RG_WIDTH // RG_BLOCKS
CONV_W = 4
RG_C = 8.0
GLA_HEADS = 4
GLA_DK = (D_MODEL // 2) // GLA_HEADS
GLA_DV = D_MODEL // GLA_HEADS
GLA_RANK = 16
GLA_TAU = 16.0
GLA_CHUNK = 64
EVEN_SPLITS = (RG_WIDTH, RG_WIDTH, GLA_HEADS * GLA_DK, GLA_HEADS * GLA_DK,
               GLA_HEADS * GLA_DV, GLA_HEADS * GLA_DV, GLA_RANK)
EVEN_OFFSETS = tuple(int(o) for o in np.cumsum(EVEN_SPLITS)[:-1])
EVEN_IN = sum(EVEN_SPLITS)
EVEN_MIX = RG_WIDTH + GLA_HEADS * GLA_DV
MLA_HEADS = 8
MLA_NOPE = 128
MLA_ROPE = 64
MLA_V = 128
MLA_Q_RANK = 256
MLA_KV_RANK = 128
MLA_QBLOCK = 128
ROPE_THETA = 10000.0
ODD_IN = MLA_Q_RANK + MLA_KV_RANK + MLA_ROPE
N_EVEN = (DEPTH + 1) // 2
N_ODD = DEPTH // 2


F32 = jnp.float32

def layer_norm(x, g, b):
    xf = x.astype(F32)
    mu = jnp.mean(xf, -1, keepdims=True)
    var = jnp.mean(jnp.square(xf - mu), -1, keepdims=True)
    return ((xf - mu) * lax.rsqrt(var + LN_EPS) * g + b).astype(x.dtype)

def rms_norm(x, g):
    xf = x.astype(F32)
    return (xf * lax.rsqrt(jnp.mean(xf * xf, -1, keepdims=True) + LN_EPS) * g).astype(x.dtype)

def modulate_2(x, shift, scale):
    return x * (1 + scale[:, None, :]) + shift[:, None, :]

def deepnorm_residual(x, f, gate, g, b, weight=1.0):
    return layer_norm(DN_ALPHA * x + weight * (1 + gate[:, None, :]) * f, g, b)

def swiglu_2(u, w_in, w_out):
    gate, up = jnp.split(u @ w_in, 2, axis=-1)
    return (jax.nn.silu(gate) * up) @ w_out

def causal_depthwise_conv(x, w, b):
    C = x.shape[-1]
    y = lax.conv_general_dilated(x, w[:, None, :], window_strides=(1,),
                                 padding=[(CONV_W - 1, 0)],
                                 dimension_numbers=('NWC', 'WIO', 'NWC'),
                                 feature_group_count=C)
    return y + b

def rg_lru(x, w_a, b_a, w_x, b_x, lam):
    B_, S, C = x.shape
    xb = x.reshape(B_, S, RG_BLOCKS, RG_BLOCK)
    r = jax.nn.sigmoid(jnp.einsum('bsni,nij->bsnj', xb, w_a).reshape(B_, S, C) + b_a)
    i = jax.nn.sigmoid(jnp.einsum('bsni,nij->bsnj', xb, w_x).reshape(B_, S, C) + b_x)
    log_a = -RG_C * r.astype(F32) * jax.nn.softplus(-lam.astype(F32))
    a = jnp.exp(log_a)
    u = jnp.sqrt(-jnp.expm1(2.0 * log_a)) * (i * x).astype(F32)

    def combine(left, right):
        a1, b1 = left
        a2, b2 = right
        return a1 * a2, a2 * b1 + b2

    _, h = lax.associative_scan(combine, (a, u), axis=1)
    return h.astype(x.dtype)

def gla_chunked(q, k, v, log_alpha):
    B_, S, H, DK = q.shape
    DV = v.shape[-1]
    C = GLA_CHUNK
    N = S // C

    def chunk(t):
        return t.astype(F32).reshape(B_, N, C, H, t.shape[-1]).transpose(0, 1, 3, 2, 4)

    qc, kc, vc = chunk(q), chunk(k), chunk(v)
    bc = jnp.cumsum(chunk(log_alpha), axis=3)
    b_last = bc[..., -1:, :]
    q_dec = qc * jnp.exp(bc)
    k_inv = kc * jnp.exp(-bc)
    k_end = kc * jnp.exp(b_last - bc)
    mask = jnp.tril(jnp.ones((C, C), dtype=bool))
    scores = jnp.where(mask, jnp.einsum('bnhid,bnhjd->bnhij', q_dec, k_inv), 0.0)
    o_intra = jnp.einsum('bnhij,bnhjv->bnhiv', scores, vc)

    def step(state, inp):
        q_n, k_n, v_n, dec_n = inp
        o = jnp.einsum('bhcd,bhdv->bhcv', q_n, state)
        state = dec_n[..., None] * state + jnp.einsum('bhcd,bhcv->bhdv', k_n, v_n)
        return state, o

    s0 = jnp.zeros((B_, H, DK, DV), F32)
    xs = (q_dec.swapaxes(0, 1), k_end.swapaxes(0, 1), vc.swapaxes(0, 1),
          jnp.exp(b_last[..., 0, :]).swapaxes(0, 1))
    _, o_inter = lax.scan(step, s0, xs)
    o = o_intra + o_inter.swapaxes(0, 1)
    return o.transpose(0, 1, 3, 2, 4).reshape(B_, S, H, DV)

def even_mixer_2(u, w_in, conv_w, conv_b, rg_wa, rg_ba, rg_wx, rg_bx, rg_lam,
               gla_wa2, gla_ba, gla_norm_g, w_out):
    B_, S, _ = u.shape
    xa, ga, q, k, v, g, za = jnp.split(u @ w_in, EVEN_OFFSETS, axis=-1)
    xa = causal_depthwise_conv(xa, conv_w, conv_b)
    ya = rg_lru(xa, rg_wa, rg_ba, rg_wx, rg_bx, rg_lam) * jax.nn.gelu(ga)
    log_alpha = jax.nn.log_sigmoid((za @ gla_wa2 + gla_ba).astype(F32)) / GLA_TAU
    o = gla_chunked(q.reshape(B_, S, GLA_HEADS, GLA_DK) * (GLA_DK ** -0.5),
                    k.reshape(B_, S, GLA_HEADS, GLA_DK),
                    v.reshape(B_, S, GLA_HEADS, GLA_DV),
                    log_alpha.reshape(B_, S, GLA_HEADS, GLA_DK))
    yb = rms_norm(o, gla_norm_g).reshape(B_, S, GLA_HEADS * GLA_DV).astype(u.dtype) * jax.nn.silu(g)
    return jnp.concatenate([ya, yb], axis=-1) @ w_out

def rope_tables(positions):
    half = MLA_ROPE // 2
    freqs = ROPE_THETA ** (-jnp.arange(half, dtype=F32) / half)
    ang = positions.astype(F32)[..., None] * freqs
    return jnp.cos(ang)[:, :, None, :], jnp.sin(ang)[:, :, None, :]

def apply_rope(x, cos, sin):
    half = MLA_ROPE // 2
    x1, x2 = x[..., :half].astype(F32), x[..., half:].astype(F32)
    return jnp.concatenate([x1 * cos - x2 * sin, x2 * cos + x1 * sin], -1).astype(x.dtype)

def causal_block_attention(q, k, v):
    B_, S, H, Dqk = q.shape
    scale = Dqk ** -0.5
    nblk = S // MLA_QBLOCK
    qb = q.reshape(B_, nblk, MLA_QBLOCK, H, Dqk).swapaxes(0, 1)
    key_idx = jnp.arange(S)

    def one_block(args):
        q_blk, blk = args
        s = jnp.einsum('bqhd,bkhd->bhqk', q_blk, k).astype(F32) * scale
        q_idx = blk * MLA_QBLOCK + jnp.arange(MLA_QBLOCK)
        s = jnp.where(key_idx[None, :] <= q_idx[:, None], s, -jnp.inf)
        p = jax.nn.softmax(s, axis=-1).astype(v.dtype)
        return jnp.einsum('bhqk,bkhd->bqhd', p, v)

    o = lax.map(one_block, (qb, jnp.arange(nblk)))
    return o.swapaxes(0, 1).reshape(B_, S, H, v.shape[-1])

def odd_mixer_2(u, positions, w_in, q_norm_g, w_q_up, kv_norm_g, w_kv_up, w_out):
    B_, S, _ = u.shape
    cq, ckv, k_pe = jnp.split(u @ w_in, [MLA_Q_RANK, MLA_Q_RANK + MLA_KV_RANK], axis=-1)
    q = (rms_norm(cq, q_norm_g) @ w_q_up).reshape(B_, S, MLA_HEADS, MLA_NOPE + MLA_ROPE)
    kv = (rms_norm(ckv, kv_norm_g) @ w_kv_up).reshape(B_, S, MLA_HEADS, MLA_NOPE + MLA_V)
    q_nope, q_pe = q[..., :MLA_NOPE], q[..., MLA_NOPE:]
    k_nope, v = kv[..., :MLA_NOPE], kv[..., MLA_NOPE:]
    cos, sin = rope_tables(positions)
    q_pe = apply_rope(q_pe, cos, sin)
    k_pe = apply_rope(k_pe[:, :, None, :], cos, sin)
    q = jnp.concatenate([q_nope, q_pe], -1)
    k = jnp.concatenate([k_nope, jnp.broadcast_to(k_pe, (B_, S, MLA_HEADS, MLA_ROPE))], -1)
    o = causal_block_attention(q, k, v)
    return o.reshape(B_, S, MLA_HEADS * MLA_V) @ w_out

def second_inputs(seed: int = 0) -> dict:
    key = jax.random.key(seed)
    ks = iter(jax.random.split(key, 40))
    nrm = lambda shape, s: jax.random.normal(next(ks), shape, F32) * s
    x = jax.random.normal(next(ks), (BATCH, SEQ, D_MODEL), F32)
    c = jax.random.normal(next(ks), (BATCH, D_MODEL), F32)
    offs = jax.random.randint(next(ks), (BATCH, 1), 0, 1024, dtype=jnp.int32)
    positions = jnp.arange(SEQ, dtype=jnp.int32)[None, :] + offs
    mod_w = nrm((DEPTH, D_MODEL, N_MOD * D_MODEL), 0.1 * D_MODEL ** -0.5)
    mod_b = nrm((DEPTH, N_MOD * D_MODEL), 0.01)
    ffn_in = nrm((DEPTH, 2, D_MODEL, 2 * D_FF), D_MODEL ** -0.5)
    ffn_out = nrm((DEPTH, 2, D_FF, D_MODEL), DN_BETA * D_FF ** -0.5)
    ln_g = 1.0 + nrm((DEPTH, 3, D_MODEL), 0.02)
    ln_b = nrm((DEPTH, 3, D_MODEL), 0.02)
    even_w_in = nrm((N_EVEN, D_MODEL, EVEN_IN), D_MODEL ** -0.5)
    conv_w = nrm((N_EVEN, CONV_W, RG_WIDTH), CONV_W ** -0.5)
    conv_b = nrm((N_EVEN, RG_WIDTH), 0.01)
    rg_wa = nrm((N_EVEN, RG_BLOCKS, RG_BLOCK, RG_BLOCK), RG_BLOCK ** -0.5)
    rg_ba = nrm((N_EVEN, RG_WIDTH), 0.01)
    rg_wx = nrm((N_EVEN, RG_BLOCKS, RG_BLOCK, RG_BLOCK), RG_BLOCK ** -0.5)
    rg_bx = nrm((N_EVEN, RG_WIDTH), 0.01)
    a_c = jax.random.uniform(next(ks), (N_EVEN, RG_WIDTH), F32, 0.9, 0.999)
    a0 = a_c ** (1.0 / RG_C)
    rg_lam = jnp.log(a0) - jnp.log1p(-a0)
    gla_wa2 = nrm((N_EVEN, GLA_RANK, GLA_HEADS * GLA_DK), GLA_RANK ** -0.5)
    gla_ba = nrm((N_EVEN, GLA_HEADS * GLA_DK), 0.1)
    gla_norm_g = 1.0 + nrm((N_EVEN, GLA_DV), 0.02)
    even_w_out = nrm((N_EVEN, EVEN_MIX, D_MODEL), DN_BETA * EVEN_MIX ** -0.5)
    odd_w_in = nrm((N_ODD, D_MODEL, ODD_IN), D_MODEL ** -0.5)
    q_norm_g = 1.0 + nrm((N_ODD, MLA_Q_RANK), 0.02)
    w_q_up = nrm((N_ODD, MLA_Q_RANK, MLA_HEADS * (MLA_NOPE + MLA_ROPE)), MLA_Q_RANK ** -0.5)
    kv_norm_g = 1.0 + nrm((N_ODD, MLA_KV_RANK), 0.02)
    w_kv_up = nrm((N_ODD, MLA_KV_RANK, MLA_HEADS * (MLA_NOPE + MLA_V)), MLA_KV_RANK ** -0.5)
    odd_w_out = nrm((N_ODD, MLA_HEADS * MLA_V, D_MODEL), DN_BETA * (MLA_HEADS * MLA_V) ** -0.5)
    return {"x": x, "c": c, "positions": positions, "mod_w": mod_w, "mod_b": mod_b,
            "ffn_in": ffn_in, "ffn_out": ffn_out, "ln_g": ln_g, "ln_b": ln_b,
            "even_w_in": even_w_in, "conv_w": conv_w, "conv_b": conv_b,
            "rg_wa": rg_wa, "rg_ba": rg_ba, "rg_wx": rg_wx, "rg_bx": rg_bx, "rg_lam": rg_lam,
            "gla_wa2": gla_wa2, "gla_ba": gla_ba, "gla_norm_g": gla_norm_g,
            "even_w_out": even_w_out, "odd_w_in": odd_w_in, "q_norm_g": q_norm_g,
            "w_q_up": w_q_up, "kv_norm_g": kv_norm_g, "w_kv_up": w_kv_up,
            "odd_w_out": odd_w_out}

def second_block(x, c, positions, mod_w, mod_b, ffn_in, ffn_out, ln_g, ln_b,
              even_w_in, conv_w, conv_b, rg_wa, rg_ba, rg_wx, rg_bx, rg_lam,
              gla_wa2, gla_ba, gla_norm_g, even_w_out, odd_w_in, q_norm_g,
              w_q_up, kv_norm_g, w_kv_up, odd_w_out):
    c_act = jax.nn.silu(c)
    for l in range(DEPTH):
        mod = c_act @ mod_w[l] + mod_b[l]
        sh1, sc1, g1, sh2, sc2, g2, sh3, sc3, g3 = jnp.split(mod, N_MOD, axis=-1)
        f = swiglu_2(modulate_2(x, sh1, sc1), ffn_in[l, 0], ffn_out[l, 0])
        x = deepnorm_residual(x, f, g1, ln_g[l, 0], ln_b[l, 0], 0.5)
        u = modulate_2(x, sh2, sc2)
        if l % 2 == 0:
            e = l // 2
            m = even_mixer_2(u, even_w_in[e], conv_w[e], conv_b[e], rg_wa[e], rg_ba[e],
                           rg_wx[e], rg_bx[e], rg_lam[e], gla_wa2[e], gla_ba[e],
                           gla_norm_g[e], even_w_out[e])
        else:
            o = l // 2
            m = odd_mixer_2(u, positions, odd_w_in[o], q_norm_g[o], w_q_up[o],
                          kv_norm_g[o], w_kv_up[o], odd_w_out[o])
        x = deepnorm_residual(x, m, g2, ln_g[l, 1], ln_b[l, 1])
        f = swiglu_2(modulate_2(x, sh3, sc3), ffn_in[l, 1], ffn_out[l, 1])
        x = deepnorm_residual(x, f, g3, ln_g[l, 2], ln_b[l, 2], 0.5)
    return x


def setup_inputs(seed=0):
    out = dict(first_inputs(seed))
    for name, value in second_inputs(seed + 1).items():
        if name != "x":
            out[name + "_2"] = value
    return out


def reference(
    x, c, ctx, c_ctx, ada_w, ada_b, norm_g, ffn1_w_gu, ffn1_w_down, ffn2_w_gu, ffn2_w_down,
    e_w_in, e_mu, e_w0, e_w_up, e_a0, e_a_up, e_g_up, e_k_k, e_k_a, e_r_k, e_gn_w, e_gn_b,
    e_w_out, o_w_in, o_conv_w, o_conv_b, o_cnorm_g, o_pool_w, o_pool_scale, o_w_out, final_g,
    c_2, positions_2, mod_w_2, mod_b_2, ffn_in_2, ffn_out_2, ln_g_2, ln_b_2, even_w_in_2,
    conv_w_2, conv_b_2, rg_wa_2, rg_ba_2, rg_wx_2, rg_bx_2, rg_lam_2, gla_wa2_2, gla_ba_2,
    gla_norm_g_2, even_w_out_2, odd_w_in_2, q_norm_g_2, w_q_up_2, kv_norm_g_2, w_kv_up_2,
    odd_w_out_2,
):
    x = first_block(
        x, c, ctx, c_ctx, ada_w, ada_b, norm_g, ffn1_w_gu, ffn1_w_down, ffn2_w_gu, ffn2_w_down,
        e_w_in, e_mu, e_w0, e_w_up, e_a0, e_a_up, e_g_up, e_k_k, e_k_a, e_r_k, e_gn_w, e_gn_b,
        e_w_out, o_w_in, o_conv_w, o_conv_b, o_cnorm_g, o_pool_w, o_pool_scale, o_w_out,
        final_g,
    )
    return second_block(
        x, c_2, positions_2, mod_w_2, mod_b_2, ffn_in_2, ffn_out_2, ln_g_2, ln_b_2, even_w_in_2,
        conv_w_2, conv_b_2, rg_wa_2, rg_ba_2, rg_wx_2, rg_bx_2, rg_lam_2, gla_wa2_2, gla_ba_2,
        gla_norm_g_2, even_w_out_2, odd_w_in_2, q_norm_g_2, w_q_up_2, kv_norm_g_2, w_kv_up_2,
        odd_w_out_2,
    )


_drawn_inputs = setup_inputs


def setup_inputs(seed=0):
    import zlib

    import numpy as np

    out = dict(_drawn_inputs(seed))
    spreads = {}
    factors = {'ctx': 3.627,
     'c_ctx': 5.616,
     'e_k_k': 6.907,
     'e_gn_w': 6.038,
     'e_gn_b': 8.0,
     'o_conv_b': 8.0,
     'o_cnorm_g': 4.989,
     'o_pool_scale': 3.985,
     'mod_b_2': 4.684,
     'conv_b_2': 8.0,
     'rg_ba_2': 31.733,
     'rg_bx_2': 8.0,
     'gla_wa2_2': 3.402,
     'gla_ba_2': 8.0,
     'gla_norm_g_2': 8.0,
     'q_norm_g_2': 8.0,
     'kv_norm_g_2': 8.0}
    for name, (base, spread) in spreads.items():
        noise = np.random.default_rng([zlib.crc32(name.encode()), seed]).standard_normal(out[name].shape)
        drawn = base * np.exp(spread * noise) if base else spread * noise
        out[name] = __import__('jax').numpy.asarray(drawn.astype(out[name].dtype))
    for name, factor in factors.items():
        out[name] = (out[name] * factor).astype(out[name].dtype)
    return out
```

```python
from contextlib import ExitStack

import numpy as np

import concourse.bass as bass
from concourse import mybir

ALU = mybir.AluOpType
ACT = mybir.ActivationFunctionType
AX = mybir.AxisListType
F32 = mybir.dt.float32
I32 = mybir.dt.int32

P = 128
D = 1024
DT = D // P
S = 256
FF = 2816
FT = FF // P
PAIRS = FT // 2
NMOD = 9
ADA_COLS = 512
ADA_CHUNKS = NMOD * D // ADA_COLS
SLOT = FT * 2 * P
HD = 64
RT = 6
ALPHA = 4.0 ** 0.25
TWO_PI = 2.0 * np.pi

VEC_LIST = [("c", 8), ("c_ctx", 8), ("c_2", 8), ("norm_g", 48), ("final_g", 8), ("ada_b", 144), ("mod_b_2", 144),
            ("ln_g_2", 48), ("ln_b_2", 48),
            ("e_mu", 20), ("e_w0", 12), ("e_a0", 12), ("e_k_k", 6), ("e_k_a", 6), ("e_r_k", 6), ("e_gn_w", 6),
            ("e_gn_b", 6), ("o_conv_w", 186), ("o_conv_b", 6), ("o_cnorm_g", 6), ("o_pool_scale", 2),
            ("conv_w_2", 32), ("conv_b_2", 8), ("rg_ba_2", 8), ("rg_bx_2", 8), ("rg_lam_2", 8), ("gla_ba_2", 4),
            ("gla_norm_g_2", 2), ("q_norm_g_2", 2), ("kv_norm_g_2", 1)]
VEC_AT = {}
_n = 0
for _name, _rows in VEC_LIST:
    VEC_AT[_name] = _n
    _n += _rows
VEC_ROWS = _n
AR = 16384
VEC_TILES = -(-VEC_ROWS // P)
VEC_LOADS = sum((VEC_AT[_name] + _rows - 1) // P - VEC_AT[_name] // P + 1 for _name, _rows in VEC_LIST)


def constant_table():
    parts, at, n = [], {}, 0

    def add(name, a):
        nonlocal n
        full = np.zeros((P, a.shape[1]), np.float32)
        full[:a.shape[0]] = a
        parts.append(full)
        at[name] = (n, a.shape[1])
        n += a.shape[1]

    add("ident", np.eye(P))
    add("ones", np.ones((P, P)))
    half = np.kron(np.eye(2), np.ones((HD, HD)))
    add("half", half)
    a = 2 * np.pi * np.outer(np.arange(HD), np.arange(HD)) / HD
    add("four_c", np.concatenate([np.kron(np.eye(2), np.cos(a)), np.kron(np.eye(2), np.sin(a))], 1) / np.sqrt(S * HD))
    b = 2 * np.pi * (np.outer(np.arange(S), np.arange(S)) % S) / S
    four_n = np.concatenate([np.cos(b)[:P], np.cos(b)[P:], -np.sin(b)[:P], -np.sin(b)[P:]], 1)
    pool = []
    for w in (2, 4, 8, 16):
        m = np.zeros((S, S))
        for t in range(S):
            lo, hi = max(t - w // 2, 0), min(t + (w - 1 - w // 2), S - 1)
            m[t, lo:hi + 1] = 1.0 / (hi - lo + 1)
        m = (m - np.eye(S)).T
        pool += [m[:P], m[P:]]
    i = np.arange(HD)
    for d in range(2):
        up = (i[:, None] < i[None, :]) if d == 0 else (i[:, None] > i[None, :])
        blk = (i[:, None] // 8) == (i[None, :] // 8)
        for name, m in (("strict", up), ("incl", up | np.eye(HD, dtype=bool)), ("nincl", up | np.eye(HD, dtype=bool)), ("nblk", up & blk), ("noff", up & ~blk),
                        ("mblk", up.T & blk)):
            sign = 1.0 if name in ("strict", "incl") else -1.0
            add(f"{name}{d}", np.concatenate([m, m], 0) * sign)
    add("eye64", np.concatenate([np.eye(HD)] * 2, 0))
    reset = np.ones((P, S))
    reset[:, ::HD] = 0.0
    add("reset", reset)
    h = HD // 2
    rot = np.zeros((HD, HD))
    rot[np.arange(h) + h, np.arange(h)] = -1.0
    rot[np.arange(h), np.arange(h) + h] = 1.0
    add("rot", rot)
    f = (np.float32(10000.0) ** (-np.arange(h, dtype=np.float32) / np.float32(h))).astype(np.float32)
    add("freq", np.concatenate([f, f])[:, None])
    q = np.arange(P)
    add("causal", np.concatenate([(np.arange(S)[None] > q[:, None]) * -3.0e38,
                                  (np.arange(S)[None] > q[:, None] + P) * -3.0e38], 1))
    add("gla_mask", (i[:, None] <= i[None, :]).astype(float))
    add("eps", np.tile(np.array([[1e-6, 64e-5, 1e-5 / ALPHA ** 2, 1e-5, 1.0, 0.0, np.pi / 2]]), (P, 1)))
    at["resident"] = (0, n)
    add("four_n", four_n)
    add("pool", np.concatenate(pool, 1))
    return np.concatenate(parts, 1).astype(np.float32), at


class Chain:

    def __init__(self, eng, sem):
        self.eng, self.sem, self.n, self.extra = eng, sem, 0, None

    def __call__(self, ins):
        self.n += 1
        ins.then_inc(self.sem, 1)
        self.eng.wait_ge(self.sem, self.n if self.extra is None else self.extra + self.n)

    def loop(self, i, per_step, steps, trips):
        self.extra, self.start, self.body, self.trips = i * per_step, self.n, per_step * steps, trips

    def end(self):
        assert self.n - self.start == self.body, (self.n - self.start, self.body)
        self.n = self.start + self.body * self.trips
        self.extra = None


def steps(eng, first, end, step):
    return eng.Fori(first, end - step + 1, step)


STOP = 99


def build(nc, t, out, table_at, stop=None):
    stop = STOP if stop is None else stop
    with ExitStack() as ctx:
        def sb(name, shape, dt=F32):
            return ctx.enter_context(nc.sbuf_tensor(name, shape, dt))

        def sem(name):
            return ctx.enter_context(nc.semaphore(name))

        ncols = table_at["resident"][1]
        CT = sb("CT", [P, ncols])
        VEC = sb("VEC", [P, VEC_TILES * P])
        X = sb("X", [P, 2, DT, S])
        Y = sb("Y", [P, DT, 2 * S])
        ARENA = sb("ARENA", [P, AR])
        W = [sb(f"W{i}", [P, SLOT]) for i in range(2)]
        ADAW = sb("ADAW", [P, 2, DT, ADA_COLS])
        ACC = sb("ACC", [P, 2, 2, ADA_COLS])
        SIL = sb("SIL", [P, 2, 2 * S])
        RS = sb("RS", [P, 2 * S])
        MOD = sb("MOD", [P, 5, NMOD * DT])
        GS = sb("GS", [P, 2, DT])
        HG = sb("HG", [P, 2, DT])
        SC = sb("SC", [P, 3, DT])
        PS = [ctx.enter_context(nc.psum_tensor(f"PS{i}", [P, 512], F32)) for i in range(8)]
        ADA_PS, NORM_PS, MISC_PS = PS[4], PS[5], PS[6]

        def region(first, shape):
            n = int(np.prod(shape))
            assert first + n <= AR, (first, shape)
            a = ARENA[:, first:first + n]
            names = "abcd"[:len(shape)]
            return a if len(shape) == 1 else a.rearrange(
                f"p ({' '.join(names)}) -> p {' '.join(names)}", **dict(zip(names, shape)))

        H = region(0, [FT, 2 * S])
        SQ = Y
        PIECES = 4

        def tab(name):
            a, n = table_at[name]
            return CT[:, a:a + n]

        def vec(name, i, n=1):
            a = VEC_AT[name] + i
            return VEC[:, a:a + n]

        ident, ones = tab("ident"), tab("ones")
        eps = {e: tab("eps")[:, k:k + 1] for k, e in enumerate(("rms", "gn", "ln", "rms2", "one", "zero", "halfpi"))}

        s_vec = sem("vec_rows_loaded")
        s_tab = sem("table_loaded")
        s_x = sem("x_rows_loaded")
        s_xT = sem("x_transposed")
        s_xc = sem("x_copied")
        s_sc = sem("silu_c_ready")
        s_adaw = [sem(f"ada_weights_loaded{i}") for i in range(2)]
        s_acc = sem("ada_acc_ready")
        s_col = sem("ada_columns_summed")
        s_mod = sem("mods_copied")
        s_w = [sem(f"weights_loaded{i}") for i in range(2)]
        s_mm = sem("dense_tile_done")
        s_ev = sem("dense_tile_read")
        s_silu = sem("silu_ready")
        s_sq = sem("squares_ready")
        s_ns = sem("norm_sum_done")
        s_rs = sem("root_ready")
        s_xr = sem("x_ready")
        s_y = sem("y_ready")
        s_o = sem("out_transposed")
        s_oc = sem("out_copied")
        s_out = sem("out_written")
        s_dve = sem("vector_chain")
        s_act = sem("scalar_chain")

        plan = []
        count = {"w": 0, "t": VEC_TILES, "silu": 0}

        def ffn(gu, down, T, ada, mod, k, scale):
            tiles = 2 if T == S else 4
            sec = dict(kind="ffn", gu=gu.rearrange("(k p) n -> p k n", p=P), down=down.rearrange("(k p) n -> p k n", p=P),
                       T=T, ada=ada, w0=count["w"], t0=count["t"], silu0=count["silu"], per=tiles, mod=mod, k=k,
                       scale=scale)
            sec["ends"] = [sec["t0"] + tiles * (j + 1) for j in range(PAIRS)]
            sec["ends"] += [sec["ends"][-1] + 2 * (j + 1) for j in range(4)]
            sec["t1"] = sec["ends"][-1]
            count["w"] += PAIRS + 4
            count["t"] = sec["t1"]
            count["silu"] += FT
            plan.append(sec)
            return sec

        def proj(chunks):
            sec = dict(kind="proj", chunks=chunks, w0=count["w"], t0=count["t"])
            sec["ends"], n = [], sec["t0"]
            for _, tiles in chunks:
                n += len(tiles)
                sec["ends"].append(n)
            sec["t1"] = n
            count["w"] += len(chunks)
            count["t"] = n
            plan.append(sec)
            return sec

        f1, f2 = t["ffn1_w_gu"], t["ffn2_w_gu"]
        d1, d2 = t["ffn1_w_down"], t["ffn2_w_down"]
        fi, fo = t["ffn_in_2"], t["ffn_out_2"]

        VROWS = region(11264, [VEC_TILES, P])
        OUT = region(0, [2, D])

        ada_src = [t["ada_w"][0], t["ada_w"][1], t["mod_w_2"][0], t["mod_w_2"][1]]
        ada_src = [a.rearrange("(k p) n -> p k n", p=P) for a in ada_src]

        def wslot(c):
            return W[c % 2]

        def gate_up(c):
            a = wslot(c)[:, 0:2 * DT * 2 * P]
            return a.rearrange("p (g k n) -> p g k n", g=2, k=DT)

        def wide(c, kt, cols=2 * P):
            return wslot(c)[:, 0:kt * cols].rearrange("p (k n) -> p k n", k=kt)

        HP = 2 * HD
        R_ = region(0, [RT, S])
        V_ = region(1536, [RT, S])
        K_ = region(3072, [RT, S])
        WA = region(4608, [S])
        GD = region(4864, [S])
        U_ = region(5120, [2, S])
        KD = [region(5632 + 1536 * d, [RT, S]) for d in range(2)]
        KA = [region(8704 + 1536 * d, [RT, S]) for d in range(2)]
        Q_ = [region(11776 + 1560 * d, [RT, 4, HD + 1]) for d in range(2)]
        ZP = region(14896, [2, S + 2])
        P65 = region(15412, [4, HD + 1])
        SG = SIL[:, 0, :].rearrange("p (a b) -> p a b", a=2)
        TS = SIL[:, 1, 0:S]
        T1 = W[0][:, 0:1536].rearrange("p (m t) -> p m t", m=RT)
        T2 = W[1][:, 0:1536].rearrange("p (m t) -> p m t", m=RT)
        WUP = W[0][:, 1536:3072].rearrange("p (d n) -> p d n", d=2)
        YF = Y[:, :, :].rearrange("p a b -> p (a b)")
        GUP, FN = YF[:, 0:768], YF[:, 768:1792]
        PT1 = YF[:, 1792:3328].rearrange("p (m t) -> p m t", m=RT)
        PT2 = KA[0]
        F1 = KA[1].rearrange("p m t -> p (m t)")[:, 0:1024].rearrange("p (a b c) -> p a b c", a=2, b=2)
        ZO = region(11776, [DT, S])
        YO = X[:, 1, 0:RT]
        MU = sb("MU", [P, 2, 20])
        OKA = sb("OKA", [P, RT])
        WC = sb("WC", [P, 2, RT])
        ZB = sb("ZB", [P, P], mybir.dt.bfloat16)
        VC = [ACC[:, d, 0, 0:RT * HD].rearrange("p (m t) -> p m t", m=RT) for d in range(2)]

        def buf(d, i):
            a = W[d][:, 384 * i:384 * (i + 1)] if i < 14 else \
                ADAW[:, d].rearrange("p a b -> p (a b)")[:, 384 * (i - 14):384 * (i - 13)]
            return a.rearrange("p (m t) -> p m t", m=RT)

        B = [[buf(d, i) for i in range(24)] for d in range(2)]
        (E1, E2, E3, KT, RTL, KH, BH, ND, NO, MD, IMD, AK, VT, KHT, BHT, ARK, ARB, N2, N2I, M2, EXTRA, ET2I, TI,
         MST) = range(24)
        P1, M4I, DD, DTR, EE, ETR, ETI, EE2, ET2, ET4I, Q1, Q2, GG, UU = ND, MD, IMD, N2, N2I, M2, EXTRA, ND, MD, N2, \
            N2I, M2, ND, MD
        NSTEP = 13
        READS = 2 * NSTEP
        s_mix = sem("mixer_weights_loaded")
        s_shift = sem("tile_shifted")
        s_tanh = sem("tanh_ready")
        s_scan = sem("decay_scanned")
        s_kk = sem("keys_scaled")
        s_sq2 = sem("key_squares_ready")
        s_feat = sem("features_ready")
        s_ex = [sem(f"exps_ready{d}") for d in range(2)]
        s_vc = [sem(f"values_copied{d}") for d in range(2)]
        s_prep = [sem(f"chunk_prepared{d}") for d in range(2)]
        s_st = [sem(f"step_multiplied{d}") for d in range(2)]
        s_sv = [sem(f"step_read{d}") for d in range(2)]
        s_fl = [sem(f"side_product_done{d}") for d in range(2)]
        s_fa = [sem(f"side_product_read{d}") for d in range(2)]
        s_post = sem("bonus_terms_ready")
        s_pa = sem("post_activations_ready")

        def scan_over(eng, seq):
            for d in range(2):
                eng.wait_ge(s_sv[d], 4 * (seq + 1) * READS + 1)

        def rwkv_plan():
            w = t["e_w_in"][0].rearrange("(k p) n -> p k n", p=P)

            def cols(a, n=2 * P):
                return w[:, :, a:a + n]

            m = dict(pa=proj([(cols(256 * j), [0, 1]) for j in range(3, 9)] + [(cols(2304, P), [0])]))
            m["fa"] = count["t"]
            count["t"] += 27
            m["pb"] = proj([(cols(256 * j), [0, 1]) for j in range(11)])
            m["fb"] = count["t"]
            count["t"] += 27
            m["post"] = count["t"]
            count["t"] += 3 * 4 + 2 + 1
            wo = t["e_w_out"][0].rearrange("(k p) n -> p k n", p=P)
            m["pc"] = proj([(wo[:, :, 256 * j:256 * (j + 1)], [0, 1]) for j in range(4)])
            m["t1"] = count["t"]
            m["pa"]["then"] = lambda sp: rwkv_ups(sp, m["pa"]["t1"])
            m["pb"]["first"] = lambda sp: scan_over(sp, 0)
            m["pc"]["first"] = lambda sp: scan_over(sp, 1)

            def then(sp):
                rwkv_ups(sp, m["pb"]["t1"])
                sp.dma_start(GUP, t["e_g_up"][0]).then_inc(s_mix, 16)
                a, n_ = table_at["four_n"]
                sp.dma_start(FN, t["table"][:, a:a + n_]).then_inc(s_mix, 16)

            m["pb"]["then"] = then
            m.update(pe=rwkv_pe, act=rwkv_act, dve=rwkv_dve)
            return m

        def rwkv_ups(sp, t1):
            sp.wait_ge(s_mm, t1)
            sp.dma_start(WUP[0:HD], t["e_w_up"][0].rearrange("d r n -> r d n")).then_inc(s_mix, 16)
            sp.dma_start(WUP[HD:P], t["e_a_up"][0].rearrange("d r n -> r d n")).then_inc(s_mix, 16)

        def proj_pe(pe, mm, sec, rhs):
            idx = sec["t0"]
            for j, (src, tiles) in enumerate(sec["chunks"]):
                c = sec["w0"] + j
                pe.wait_ge(s_w[c % 2], 32 * (c // 2 + 1))
                kt, n_ = src.shape[1], src.shape[2]
                for q in tiles:
                    pe.wait_ge(s_ev, idx - 3)
                    x = rhs(idx - sec["t0"])
                    m_ = min(P, n_ - q * P)
                    for k in range(kt):
                        last = mm(PS[idx % 4][0:m_, 0:S], wide(c, kt, n_)[:, k, q * P:q * P + m_], x(k),
                                  start=(k == 0), stop=(k == kt - 1))
                    last.then_inc(s_mm, 1)
                    idx += 1

        def rwkv_pe(pe, mm, ph):
            m = mixers["rwkv"]
            pe.wait_ge(s_y, ph[2])
            for seq in range(2):
                sec = m["pa" if seq == 0 else "pb"]
                off = S if seq == 0 else 0
                proj_pe(pe, mm, sec, lambda i: lambda k: Y[:, k, off:off + S])
                idx = m["fa" if seq == 0 else "fb"]
                pe.wait_ge(s_tanh, seq + 1)
                pe.wait_ge(s_mix, 32 if seq == 0 else 96)
                for d in range(2):
                    for q in range(RT):
                        for h in (slice(0, HD), slice(HD, P)):
                            pe.wait_ge(s_ev, idx - 3)
                            mm(PS[idx % 4][:, 0:S], WUP[h, d, q * P:(q + 1) * P], WA[h], start=True, stop=True)\
                                .then_inc(s_mm, 1)
                            idx += 1
                pe.wait_ge(s_sq2, seq + 1)
                for g in range(3):
                    pe.wait_ge(s_ev, idx - 3)
                    mm(PS[idx % 4][:, :], tab("half"), T1[:, 2 * g:2 * g + 2, :], start=True, stop=True).then_inc(s_mm, 1)
                    idx += 1
                pe.wait_ge(s_ev, idx)
                lat = seq == 1

                def prods(bank, *pairs):
                    for b in range(2):
                        for q in range(RT):
                            h = slice(b * HD, (b + 1) * HD)
                            for n_, (lhs, rhs) in enumerate(pairs):
                                last = mm(PS[bank][h, q * HD:(q + 1) * HD], lhs[h, q], rhs[h, q], start=(n_ == 0),
                                          stop=(n_ == len(pairs) - 1))
                    return last

                class Eye:
                    def __getitem__(self, key):
                        return tab("eye64")[key[0], :]
                eye = Eye()
                base = 4 * seq * NSTEP
                with steps(pe, 0, 4, 1) as i:
                    for st in range(NSTEP):
                        for d in range(2):
                            b, o = B[d], 4 * d
                            if st == 0:
                                pe.wait_ge(s_prep[d], i + (4 * seq + 2))
                            if st == 2:
                                pe.wait_ge(s_vc[d], i + (4 * seq + 1))
                            if st in (2, 3, 4):
                                pe.wait_ge(s_fa[d], i * 3 + (12 * seq + st - 1))
                            pe.wait_ge(s_sv[d], i * READS + (4 * seq * READS + 2 * st + 1))
                            mm(PS[o][:, 0:1], ZB[:, :], ZB[:, 0:1], start=True, stop=True)
                            if st == 0:
                                prods(o, (b[BH], b[KT]))
                                last = prods(o + 1, (b[KT], b[BH]))
                            elif st == 1:
                                prods(o, (b[MD], b[ND]))
                                last = prods(o + 1, (b[ND], b[MD]))
                            elif st == 2:
                                prods(o, (b[IMD], b[N2I]))
                                last = prods(o + 1, (b[N2], b[M2]))
                            elif st == 3:
                                prods(o, (b[M4I], b[P1]))
                                last = prods(o + 1, (b[P1], b[M4I]))
                            elif st == 4:
                                prods(o, (b[DTR], b[NO]))
                                last = prods(o + 1, (b[NO], b[DTR]))
                            elif st == 5:
                                prods(o, (b[ETR], b[EE]))
                                last = prods(o + 1, (b[EE], b[ETR]))
                            elif st == 6:
                                last = prods(o, (b[EE2], b[ET2]))
                            elif st == 7:
                                last = prods(o, (b[ET4I], b[DD]))
                            elif st == 8:
                                last = prods(o, (b[ET2I], b[Q1]))
                            elif st == 9:
                                last = prods(o, (b[ETI], b[Q2]))
                            elif st == 10:
                                last = prods(o, (b[KT], b[MST]), (b[AK], b[VT]))
                            elif st == 11:
                                last = prods(o, (b[TI], b[GG]))
                            else:
                                if lat:
                                    prods(o, (b[MST], b[RTL]), (b[VT], b[ARK]), (b[UU], b[ARB]))
                                last = prods(o + 1, (b[KHT], b[VT]), (b[BHT], b[UU]))
                            last.then_inc(s_st[d], 1)
                            if st == 0:
                                prods(o + 2, (b[KH], eye)).then_inc(s_fl[d], 1)
                            elif st == 1:
                                prods(o + 3, (b[BH], eye)).then_inc(s_fl[d], 1)
                            elif st == 2:
                                prods(o + 2, (VC[d], eye)).then_inc(s_fl[d], 1)
                            elif st == 3:
                                prods(o + 3, (b[KH], b[KT]))
                            elif st == 4 and lat:
                                prods(o + 2, (b[KH], b[RTL]))
                            elif st == 6 and lat:
                                prods(o + 3, (b[BH], b[RTL]))
                scan_over(pe, seq)
            idx = m["post"]
            for r in range(3):
                if r:
                    pe.wait_ge(s_pa if r == 1 else s_post, 1)
                for g in range(3):
                    pe.wait_ge(s_ev, idx - 3)
                    src = YO if r == 0 else PT1
                    mm(PS[idx % 4][:, :], tab("half"), src[:, 2 * g:2 * g + 2, :], start=True, stop=True)\
                        .then_inc(s_mm, 1)
                    idx += 1
            pe.wait_ge(s_pa, 2)
            for g in range(3):
                pe.wait_ge(s_ev, idx - 3)
                for q in range(2):
                    last = mm(PS[idx % 4][:, q * S:(q + 1) * S], GUP[:, (2 * g + q) * P:(2 * g + q + 1) * P], GD,
                              start=True, stop=True)
                last.then_inc(s_mm, 1)
                idx += 1
            pe.wait_ge(s_ev, idx)
            for tt in range(2):
                for g in range(2):
                    last = mm(PS[idx % 4][:, g * S:(g + 1) * S], U_[:, g, tt * P:(tt + 1) * P], tab("four_c"),
                              start=True, stop=True)
                last.then_inc(s_mm, 1)
                idx += 1
            pe.wait_ge(s_ev, idx)
            for g in range(2):
                for n_, (tt, sc_) in enumerate(((0, 0), (1, 0), (0, 1), (1, 1))):
                    last = mm(PS[idx % 4][:, g * S:(g + 1) * S], F1[:, tt, g, sc_ * P:(sc_ + 1) * P],
                              FN[:, (2 * sc_ + tt) * S:(2 * sc_ + tt + 1) * S], start=(n_ == 0), stop=(n_ == 3))
            last.then_inc(s_mm, 1)
            pe.wait_ge(s_ev, m["pc"]["t0"])
            proj_pe(pe, mm, m["pc"], lambda i: lambda k: ZO[:, k])

        def rwkv_act(act, A, link, ph):
            m = mixers["rwkv"]
            nsh = 0
            for seq in range(2):
                sec = m["pa" if seq == 0 else "pb"]
                n_tiles = sec["t1"] - sec["t0"]
                for i in range(n_tiles):
                    idx = sec["t0"] + i
                    act.wait_ge(s_mm, idx + 1)
                    if seq == 1 and i >= 20:
                        A(U_[:, i - 20], PS[idx % 4][:, 0:S], ACT.Copy).then_inc(s_ev, 1)
                        continue
                    act.wait_ge(s_shift, max(nsh, 1))
                    nsh += 1
                    A(ZP[:, nsh % 2, 1:S + 1], PS[idx % 4][:, 0:S], ACT.Copy).then_inc(s_ev, 1)
                act.wait_ge(s_shift, nsh + 1)
                A(WA[0:HD], WA[0:HD], ACT.Tanh).then_inc(s_tanh, 1)
                idx = m["fa" if seq == 0 else "fb"]
                for d in range(2):
                    for q in range(RT):
                        i = 12 * seq + 6 * d + q
                        act.wait_ge(s_mm, idx + 1)
                        if i >= 2:
                            act.wait_ge(s_scan, i - 1)
                        A(SG[:, i % 2], PS[idx % 4][:, 0:S], ACT.Sigmoid, bias=vec("e_w0", RT * d + q))\
                            .then_inc(s_ev, 1)
                        act.wait_ge(s_mm, idx + 2)
                        A(KA[d][:, q], PS[(idx + 1) % 4][:, 0:S], ACT.Sigmoid, bias=vec("e_a0", RT * d + q))\
                            .then_inc(s_ev, 1)
                        idx += 2
                act.wait_ge(s_kk, seq + 1)
                A(T1, K_, ACT.Square).then_inc(s_sq2, 1)
                for g in range(3):
                    act.wait_ge(s_mm, idx + 1)
                    A(T2[:, 2 * g:2 * g + 2], PS[idx % 4][:, :].rearrange("p (a b) -> p a b", a=2), ACT.Sqrt)\
                        .then_inc(s_ev, 1)
                    idx += 1
                act.wait_ge(s_feat, seq + 1)

                def ps(k):
                    return PS[k][:, 0:RT * HD].rearrange("p (m t) -> p m t", m=RT)

                with steps(act, 0, 4, 1) as i:
                    for d in range(2):
                        c = i if d == 0 else i * (-1) + 3
                        act.wait_ge(s_prep[d], i + (4 * seq + 1))
                        qf = Q_[d].rearrange("p m c e -> p m (c e)")
                        off = c * (HD + 1)

                        def sl(first):
                            return qf[:, :, bass.ds(off + first, HD)]
                        f_ex, f_inc = (0, 1) if d == 0 else (1, 0)
                        A(B[d][E1], sl(f_ex), ACT.Exp)
                        A(B[d][E2], sl(f_inc), ACT.Exp)
                        A(B[d][E3], sl(f_inc), ACT.Exp, scale=-1.0).then_inc(s_ex[d], 1)
                    for d in range(2):
                        c = i if d == 0 else i * (-1) + 3
                        A(VC[d], V_[:, :, bass.ds(c * HD, HD)], ACT.Copy).then_inc(s_vc[d], 1)
                    for st in range(6):
                        for d in range(2):
                            b, o = B[d], 4 * d
                            if st:
                                act.wait_ge(s_st[d], i * NSTEP + (4 * seq * NSTEP + st + 1))
                                dst, bank = {1: (M2, o + 1), 2: (P1, o), 3: (DD, o), 4: (EE, o), 5: (EE2, o)}[st]
                                A(b[dst], ps(bank), ACT.Copy).then_inc(s_sv[d], 1)
                            if st < 3:
                                act.wait_ge(s_fl[d], i * 3 + (12 * seq + st + 1))
                                dst, bank, sign = ((KHT, o + 2, 1.0), (BHT, o + 3, -1.0), (VT, o + 2, 1.0))[st]
                                A(b[dst], ps(bank), ACT.Copy, scale=sign).then_inc(s_fa[d], 1)
                scan_over(act, seq)
            act.wait_ge(s_ev, m["post"] + 3)
            A(PT1, YO, ACT.Square).then_inc(s_pa, 1)
            idx = m["post"] + 3
            for g in range(3):
                act.wait_ge(s_mm, idx + 1)
                ins = A(PT2[:, 2 * g:2 * g + 2], PS[idx % 4][:, :].rearrange("p (a b) -> p a b", a=2), ACT.Sqrt,
                        bias=eps["gn"], scale=1.0 / HD)
                ins.then_inc(s_ev, 1)
                idx += 1
            A(GD, GD, ACT.Sigmoid).then_inc(s_pa, 1)
            idx = m["post"] + 12
            for tt in range(2):
                act.wait_ge(s_mm, idx + 1)
                A(F1[:, tt], PS[idx % 4][:, :].rearrange("p (a b) -> p a b", a=2), ACT.Copy).then_inc(s_ev, 1)
                idx += 1

        def rwkv_dve(dve, V, link, ph):
            m = mixers["rwkv"]
            DS = 0.606531
            link(V.tensor_scalar(MU[:, 0], vec("e_mu", 0, 20), -1.0, 1.0, ALU.mult, ALU.add))
            link(V.tensor_scalar(MU[:, 1], vec("e_mu", 0, 20), 0.5, None, ALU.mult))
            link(V.tensor_scalar(OKA[:, :], vec("e_k_a", 0, RT), -1.0, 1.0, ALU.mult, ALU.add))
            link(V.memset(ZB[:, :], 0.0))
            V.memset(ZP, 0.0).then_inc(s_prep[0], 1)
            V.memset(P65, 0.0).then_inc(s_prep[1], 1)
            for d in range(2):
                V.memset(B[d][MST], 0.0).then_inc(s_sv[d], 1)
            V.memset(Q_[0], 0.0).then_inc(s_shift, 1)
            dve.wait_ge(s_shift, 1)
            nsh = 0
            for seq in range(2):
                sec = m["pa" if seq == 0 else "pb"]
                kinds = list(range(6, 19)) if seq == 0 else list(range(20))
                for i, f in enumerate(kinds):
                    idx = sec["t0"] + i
                    nsh += 1
                    z = ZP[:, nsh % 2]
                    o = R_[:, f] if f < 6 else K_[:, f - 6] if f < 12 else V_[:, f - 12] if f < 18 else WA if f == 18 \
                        else GD
                    dve.wait_ge(s_ev, idx + 1)
                    link(V.tensor_tensor(TS, z[:, 0:S], z[:, 2:S + 2], ALU.add))
                    link(V.tensor_scalar(o, z[:, 1:S + 1], MU[:, 0, f:f + 1], None, ALU.mult))
                    V.scalar_tensor_tensor(o, TS, MU[:, 1, f:f + 1], o, ALU.mult, ALU.add).then_inc(s_shift, 1)
                    dve.wait_ge(s_shift, nsh + 1)
                idx = m["fa" if seq == 0 else "fb"]
                for d in range(2):
                    for q in range(RT):
                        i = 12 * seq + 6 * d + q
                        dve.wait_ge(s_ev, idx + 1)
                        link(V.tensor_tensor_scan(TS, tab("reset"), SG[:, i % 2], 0.0, ALU.mult, ALU.add))
                        ts4 = TS.rearrange("p (c e) -> p c e", c=4)
                        if d == 0:
                            V.tensor_scalar(Q_[0][:, q, :, 1:HD + 1], ts4, -DS, None, ALU.mult).then_inc(s_scan, 1)
                        else:
                            link(V.tensor_scalar(P65[:, :, 1:HD + 1], ts4, -DS, None, ALU.mult))
                            V.tensor_tensor(Q_[1][:, q], P65[:, :, HD:HD + 1].to_broadcast([P, 4, HD + 1]), P65,
                                            ALU.subtract).then_inc(s_scan, 1)
                        dve.wait_ge(s_scan, i + 1)
                        idx += 2
                dve.wait_ge(s_ev, idx)
                for d in range(2):
                    for q in range(RT):
                        ins = V.tensor_scalar(KD[d][:, q], KA[d][:, q], vec("e_k_a", q), OKA[:, q:q + 1], ALU.mult,
                                              ALU.add)
                    link(ins)
                    link(V.tensor_tensor(KD[d], KD[d], K_, ALU.mult))
                for q in range(RT):
                    ins = V.tensor_scalar(K_[:, q], K_[:, q], vec("e_k_k", q), None, ALU.mult)
                ins.then_inc(s_kk, 1)
                idx += 3
                dve.wait_ge(s_kk, seq + 1)
                dve.wait_ge(s_ev, idx)
                link(V.tensor_scalar(T2, T2, 1e-12, None, ALU.max))
                link(V.reciprocal(T2, T2))
                link(V.tensor_tensor(K_, K_, T2, ALU.mult))
                if seq == 1:
                    link(V.memset(YO, 0.0))
                V.tensor_tensor(KA[0], KA[0], K_, ALU.mult)
                V.tensor_tensor(KA[1], KA[1], K_, ALU.mult).then_inc(s_feat, 1)
                dve.wait_ge(s_feat, seq + 1)

                def mask(name, d):
                    return tab(f"{name}{d}").unsqueeze(1).to_broadcast([P, RT, HD])

                eye = tab("eye64").unsqueeze(1).to_broadcast([P, RT, HD])

                def ps(k):
                    return PS[k][:, 0:RT * HD].rearrange("p (m t) -> p m t", m=RT)

                lat = seq == 1
                base = 4 * seq * NSTEP
                with steps(dve, 0, 4, 1) as i:
                    link.loop(i, 6 if lat else 4, 1, 4)
                    for d in range(2):
                        c = (i if d == 0 else i * (-1) + 3) * HD
                        b = B[d]
                        dve.wait_ge(s_ex[d], i + (4 * seq + 1))
                        dve.wait_ge(s_sv[d], i * READS + (4 * seq * READS + 1))
                        V.tensor_tensor(b[KT], K_[:, :, bass.ds(c, HD)], b[E1], ALU.mult)
                        if lat:
                            V.tensor_tensor(b[RTL], R_[:, :, bass.ds(c, HD)], b[E2], ALU.mult)
                        last_ = HD - 1 if d == 0 else 0
                        V.tensor_copy(WC[:, d], b[E2][:, :, last_])
                        V.tensor_tensor(b[KH], KD[d][:, :, bass.ds(c, HD)], b[E3], ALU.mult)
                        V.tensor_tensor(b[BH], KA[d][:, :, bass.ds(c, HD)], b[E3], ALU.mult).then_inc(s_prep[d], 1)
                    for st in range(NSTEP):
                        for d in range(2):
                            b, o = B[d], 4 * d
                            c = (i if d == 0 else i * (-1) + 3) * HD
                            dve.wait_ge(s_st[d], i * NSTEP + (base + st + 1))
                            if st == 0:
                                link(V.tensor_tensor(b[MD], ps(o + 1), mask("mblk", d), ALU.mult))
                                V.tensor_tensor(b[ND], ps(o), mask("nblk", d), ALU.mult)
                                V.tensor_tensor(b[NO], ps(o), mask("noff", d), ALU.mult)
                                ins = V.tensor_tensor(b[IMD], b[MD], eye, ALU.add)
                            elif st == 1:
                                V.tensor_copy(b[N2], ps(o))
                                ins = V.tensor_tensor(b[N2I], ps(o), eye, ALU.add)
                            elif st == 2:
                                ins = V.tensor_tensor(b[M4I], ps(o + 1), eye, ALU.add)
                            elif st == 3:
                                ins = V.tensor_copy(b[DTR], ps(o + 1))
                            elif st == 4:
                                V.tensor_copy(b[ETR], ps(o + 1))
                                ins = V.tensor_tensor(b[ETI], ps(o + 1), eye, ALU.add)
                            elif st == 5:
                                V.tensor_copy(b[ET2], ps(o + 1))
                                ins = V.tensor_tensor(b[ET2I], ps(o + 1), eye, ALU.add)
                            elif st == 6:
                                ins = V.tensor_tensor(b[ET4I], ps(o), eye, ALU.add)
                            elif st < 12:
                                ins = V.tensor_copy(b[{7: Q1, 8: Q2, 9: TI, 10: GG, 11: UU}[st]], ps(o))
                            else:
                                yv = YO[:, :, bass.ds(c, HD)]
                                link(V.tensor_tensor(b[MST], b[MST], ps(o + 1), ALU.add))
                                ins = V.tensor_tensor(b[MST], b[MST],
                                                      WC[:, d].unsqueeze(2).to_broadcast([P, RT, HD]), ALU.mult)
                                if lat:
                                    link(ins)
                                    ins = V.tensor_tensor(yv, yv, ps(o), ALU.add)
                            ins.then_inc(s_sv[d], 1 if 1 <= st <= 5 else 2)
                            if st == 4:
                                V.tensor_tensor(b[AK], ps(o + 3), mask("strict", d), ALU.mult)
                            elif st == 5 and lat:
                                V.tensor_tensor(b[ARK], ps(o + 2), mask("incl", d), ALU.mult)
                            elif st == 7 and lat:
                                V.tensor_tensor(b[ARB], ps(o + 3), mask("nincl", d), ALU.mult)
                    link.end()
                scan_over(dve, seq)
            idx = m["post"]
            for g in range(3):
                dve.wait_ge(s_mm, idx + 1)
                yg = YO[:, 2 * g:2 * g + 2]
                pv = PS[idx % 4][:, :].rearrange("p (a b) -> p a b", a=2)
                ins = V.scalar_tensor_tensor(yg, pv, -1.0 / HD, yg, ALU.mult, ALU.add)
                ins.then_inc(s_ev, 1)
                idx += 1
            dve.wait_ge(s_ev, idx)
            dve.wait_ge(s_ev, idx + 3)
            idx += 3
            link(V.reciprocal(PT2, PT2))
            link(V.tensor_tensor(YO, YO, PT2, ALU.mult))
            for q in range(RT):
                ins = V.tensor_scalar(YO[:, q], YO[:, q], vec("e_gn_w", q), vec("e_gn_b", q), ALU.mult, ALU.add)
            link(ins)
            link(V.tensor_tensor(PT1, KD[0], KD[1], ALU.add))
            link(V.tensor_tensor(PT1, PT1, R_, ALU.mult))
            for q in range(RT):
                ins = V.tensor_scalar(PT1[:, q], PT1[:, q], vec("e_r_k", q), None, ALU.mult)
            ins.then_inc(s_post, 1)
            dve.wait_ge(s_post, 1)
            for g in range(3):
                dve.wait_ge(s_mm, idx + 1)
                pv = PS[idx % 4][:, :].rearrange("p (a b) -> p a b", a=2)
                V.tensor_tensor(PT2[:, 2 * g:2 * g + 2], V_[:, 2 * g:2 * g + 2], pv, ALU.mult).then_inc(s_ev, 1)
                idx += 1
            dve.wait_ge(s_ev, idx)
            link(V.tensor_tensor(YO, YO, PT2, ALU.add))
            for g in range(3):
                dve.wait_ge(s_mm, idx + 1)
                pv = PS[idx % 4][:, :].rearrange("p (a b) -> p a b", a=2)
                V.tensor_tensor(ZO[:, 2 * g:2 * g + 2], YO[:, 2 * g:2 * g + 2], pv, ALU.mult).then_inc(s_ev, 1)
                idx += 1
            idx += 2
            dve.wait_ge(s_mm, idx + 1)
            V.tensor_copy(ZO[:, 6:8], PS[idx % 4][:, :].rearrange("p (a b) -> p a b", a=2)).then_inc(s_ev, 1)
            idx += 1
            dve.wait_ge(s_ev, idx)
            proj_add(dve, V, m["pc"])

        def proj_add(dve, V, sec):
            for i in range(DT):
                idx = sec["t0"] + i
                dve.wait_ge(s_mm, idx + 1)
                V.scalar_tensor_tensor(X[:, 0, i], PS[idx % 4][:, 0:S], HG[:, 0, i:i + 1], X[:, 0, i], ALU.mult,
                                       ALU.add).then_inc(s_ev, 1)
            dve.wait_ge(s_ev, sec["t1"])

        CW, CT_ = 31, 6
        UP = region(0, [CT_, S + CW - 1])
        CO = region(1716, [CT_, S])
        ZC = region(3328, [DT, S])
        PQ = region(5376, [2, S])
        POOLW = region(5888, [2, HD])
        QM = region(6016, [2, S])
        POOLM = region(6528, [4, 2, S])
        SQC = region(8704, [CT_, S])
        VTAPS = 16
        PTAPS = CW - VTAPS
        DIAG = region(10240, [3, PTAPS, P])
        s_dg = sem("tap_diagonals_ready")
        s_cw = sem("pool_tables_loaded")
        s_sg = sem("gate_sigmoid_ready")
        s_cz = sem("conv_branch_ready")

        def conv_plan():
            w = t["o_w_in"][0].rearrange("(k p) n -> p k n", p=P)

            def cols(a):
                return w[:, :, a:a + 2 * P]

            m = dict(pin=proj([(cols(c), [0, 1]) for j in range(3) for c in (256 * j, 768 + 256 * j)]
                              + [(cols(1536), [0, 1])]))
            m["cv"] = count["t"]
            m["mid"] = m["cv"] + CT_
            count["t"] = m["mid"] + 4 + 4
            wo = t["o_w_out"][0].rearrange("(k p) n -> p k n", p=P)
            m["pout"] = proj([(wo[:, :, 256 * j:256 * (j + 1)], [0, 1]) for j in range(4)])
            m["t1"] = count["t"]

            def first(sp):
                sp.wait_ge(s_ev, m["pin"]["t0"])
                for g in range(4):
                    sp.dma_start(POOLW[(g % 2) * HD:(g % 2 + 1) * HD, g // 2], t["o_pool_w"][0, g]).then_inc(s_cw, 16)
                a, n_ = table_at["pool"]
                sp.dma_start(POOLM.rearrange("p a b c -> p (a b c)"), t["table"][:, a:a + n_]).then_inc(s_cw, 16)

            m["pin"]["first"] = first
            m["phases"] = conv_phases
            return m

        def conv_phases(layer):
            m = mixers["conv"]
            sec, mid = m["pin"], m["mid"]
            n_y = n["y"]

            def pe1(pe, mm):
                pe.wait_ge(s_y, n_y)
                proj_pe(pe, mm, sec, lambda i: lambda k: Y[:, k, 0:S])
                idx = m["cv"]
                pe.wait_ge(s_ev, idx)
                for f in range(CT_):
                    pe.wait_ge(s_dg, f + 1)
                    if f >= 4:
                        pe.wait_ge(s_ev, idx - 3)
                    for k in range(PTAPS):
                        last = mm(PS[idx % 4][:, 0:S], DIAG[:, f % 3, k], UP[:, f, VTAPS + k:VTAPS + k + S],
                                  start=(k == 0), stop=(k == PTAPS - 1))
                    last.then_inc(s_mm, 1)
                    idx += 1

            def act1(act, A, link):
                def diagonals(f):
                    if f >= 3:
                        act.wait_ge(s_mm, m["cv"] + f - 2)
                    for k in range(PTAPS):
                        last = A(DIAG[:, f % 3, k], ident, ACT.Copy, scale=vec("o_conv_w", CT_ * (VTAPS + k) + f))
                    last.then_inc(s_dg, 1)

                act.wait_ge(s_ev, sec["t0"])
                for f in range(3):
                    diagonals(f)
                for f in range(CT_):
                    idx = sec["t0"] + 4 * (f // 2) + 2 + f % 2
                    act.wait_ge(s_mm, idx + 1)
                    if f >= 2:
                        act.wait_ge(s_ev, idx - (5, 3)[f % 2])
                    A(SIL[:, f % 2, 0:S], PS[idx % 4][:, 0:S], ACT.Sigmoid).then_inc(s_sg, 1)
                for f in range(3, CT_):
                    diagonals(f)

            def dve1(dve, V, link):
                link(V.memset(UP, 0.0))
                for f in range(CT_):
                    idx = sec["t0"] + 4 * (f // 2) + f % 2
                    dve.wait_ge(s_mm, idx + 1)
                    dve.wait_ge(s_sg, f + 1)
                    V.tensor_tensor(UP[:, f, CW // 2:CW // 2 + S], SIL[:, f % 2, 0:S], PS[idx % 4][:, 0:S], ALU.mult)\
                        .then_inc(s_ev, 1 if f % 2 == 0 else 3)
                for q in range(2):
                    idx = sec["t0"] + 12 + q
                    dve.wait_ge(s_mm, idx + 1)
                    V.tensor_copy(PQ[:, q], PS[idx % 4][:, 0:S]).then_inc(s_ev, 1)
                dve.wait_ge(s_ev, sec["t1"])
                for f in range(CT_):
                    ins = V.tensor_scalar(CO[:, f], UP[:, f, 0:S], vec("o_conv_w", f), vec("o_conv_b", f), ALU.mult,
                                          ALU.add)
                for k in range(1, VTAPS):
                    link(ins)
                    for f in range(CT_):
                        ins = V.scalar_tensor_tensor(CO[:, f], UP[:, f, k:k + S], vec("o_conv_w", CT_ * k + f), CO[:, f],
                                                     ALU.mult, ALU.add)
                link(ins)
                for f in range(CT_):
                    dve.wait_ge(s_mm, m["cv"] + f + 1)
                    V.tensor_tensor(CO[:, f], CO[:, f], PS[(m["cv"] + f) % 4][:, 0:S], ALU.add).then_inc(s_ev, 1)
                dve.wait_ge(s_ev, m["mid"])

            add("do", pe1, act1, dve1)
            add("squares", [CO], [SQC], [(s_ev, mid)])
            add("sum", S, SQC, CT_, [bump("sq")], n["rs"])
            add("root", S, 1.0 / 768, "rms", bump("ns"), n["y"], n["x"])
            n_rs = bump("rs")
            n_u = bump("x")

            def pe2(pe, mm):
                idx = mid
                pe.wait_ge(s_cw, 80)
                pe.wait_ge(s_ev, mid)
                for tt in range(2):
                    for par in range(2):
                        pe.wait_ge(s_ev, idx - 3)
                        h = slice(par * HD, (par + 1) * HD)
                        for g2 in range(2):
                            last = mm(PS[idx % 4][:, g2 * HD:(g2 + 1) * HD], PQ[h, g2, tt * P:(tt + 1) * P],
                                      POOLW[h, g2], start=True, stop=True)
                        last.then_inc(s_mm, 1)
                        idx += 1
                pe.wait_ge(s_ev, idx)
                for g in range(4):
                    pe.wait_ge(s_ev, idx - 3)
                    h = slice((g % 2) * HD, (g % 2 + 1) * HD)
                    for tt in range(2):
                        last = mm(PS[idx % 4][h, 0:S], QM[:, tt, g * HD:(g + 1) * HD], POOLM[:, g, tt],
                                  start=(tt == 0), stop=(tt == 1))
                    last.then_inc(s_mm, 1)
                    idx += 1
                pe.wait_ge(s_ev, idx)
                pe.wait_ge(s_cz, 1)
                proj_pe(pe, mm, m["pout"], lambda i: lambda k: ZC[:, k])

            def act2(act, A, link):
                act.wait_ge(s_xr, n_u)
                for f in range(CT_):
                    last = A(ZC[:, f], CO[:, f], ACT.Silu, scale=vec("o_cnorm_g", f))
                last.then_inc(s_cz, 1)

            def dve2(dve, V, link):
                dve.wait_ge(s_rs, n_rs)
                link(V.reciprocal(RS[:, 0:S], RS[:, 0:S]))
                V.tensor_tensor(CO, CO, RS[:, 0:S].unsqueeze(1).to_broadcast([P, CT_, S]), ALU.mult).then_inc(s_xr, 1)
                idx = mid
                for tt in range(2):
                    for par in range(2):
                        dve.wait_ge(s_mm, idx + 1)
                        q = QM[:, tt].rearrange("p (g two c) -> p g two c", g=2, two=2)
                        V.tensor_copy(q[:, :, par], PS[idx % 4][:, 0:P].rearrange("p (g c) -> p g c", g=2))\
                            .then_inc(s_ev, 1)
                        idx += 1
                for g in range(4):
                    h = slice((g % 2) * HD, (g % 2 + 1) * HD)
                    dve.wait_ge(s_mm, idx + 1)
                    V.tensor_scalar(ZC[h, 6 + g // 2], PS[idx % 4][h, 0:S], vec("o_pool_scale", g // 2)[h], None,
                                    ALU.mult).then_inc(s_ev, 1)
                    idx += 1
                proj_add(dve, V, m["pout"])

            add("do", pe2, act2, dve2)

        Z16 = region(0, [16, S])
        XAP = region(4096, [DT, S + 3])
        TH = region(4096, [DT, S])
        ST = region(4096, [4, 3, S])
        XC = region(6168, [DT, S])
        AR_ = region(8216, [DT, S])
        AI = region(10264, [DT, S])
        QG = region(12312, [4, S])
        KG = region(13336, [4, S])
        LA = region(14360, [4, S])
        YH = Y[:, :, S:2 * S]
        VTOK = X[:, 1].rearrange("p a b -> p (a b)").rearrange("p (t n) -> p t n", t=2)
        AF = ADAW[:, :, :, :].rearrange("p a b c -> p (a b c)")

        def spare(first, *shape):
            a = AF[:, first:first + int(np.prod(shape))]
            names = "abcd"[:len(shape)]
            return a.rearrange(f"p ({' '.join(names)}) -> p {' '.join(names)}", **dict(zip(names, shape)))

        RGW = spare(0, 2, DT, HD)
        WA2 = spare(1024, 512)
        QD, KI, KE = spare(1536, 4, S), spare(2560, 4, S), spare(3584, 4, S)
        KET = spare(4608, 2, 512)
        ZA = spare(5632, S)
        BC, DX = spare(6144, 4, S), spare(7168, 4, S)
        SCO = spare(7168, 4, 4, HD)
        RR = region(12312, [4, S])
        SPL = sb("SPL", [P, 5, DT])
        DEC = sb("DEC", [P, 4, 4])
        s_gw = sem("gla_weights_loaded")
        s_ga = sem("gla_scalar_step")

        def gla_plan():
            w = t["even_w_in_2"][0].rearrange("(k p) n -> p k n", p=P)

            def cols(a, n_=2 * P):
                return w[:, :, a:a + n_]

            pair = [0, 1]
            m = dict(p1=proj([(cols(256 * j), pair) for j in range(4)] + [(cols(5120, 16), [0])]
                             + [(cols(2048 + 256 * j), pair) for j in range(4)]))
            m["la"] = count["t"]
            m["rg"] = m["la"] + 4
            count["t"] = m["rg"] + 16
            m["pv"] = proj([(cols(3072 + 256 * j), pair) for j in range(4)])
            m["p2"] = proj([(cols(4096 + 256 * j), pair) for j in range(4)] + [(cols(1024 + 256 * j), pair) for j in range(4)])
            m["sc"] = count["t"]
            m["sq"] = m["sc"] + 1 + 2 + 8 + 8
            count["t"] = m["sq"] + 2
            wo = t["even_w_out_2"][0].rearrange("(k p) n -> p k n", p=P)
            m["pout"] = proj([(wo[:, :, 256 * j:256 * (j + 1)], pair) for j in range(4)])
            m["t1"] = count["t"]

            def first(sp):
                sp.wait_ge(s_acc, 4 * ADA_CHUNKS)
                for g, name in enumerate(("rg_wa_2", "rg_wx_2")):
                    src = t[name][0].rearrange("(f b) i j -> b i f j", b=2)
                    for b in range(2):
                        sp.dma_start(RGW[b * HD:(b + 1) * HD, g], src[b]).then_inc(s_gw, 16)
                sp.dma_start(WA2[0:16], t["gla_wa2_2"][0]).then_inc(s_gw, 16)

            m["p1"]["first"] = first
            m["phases"] = gla_phases
            return m

        def gla_phases(layer):
            m = mixers["gla"]
            n_y = n["y"]
            n_sp, n_xc, n_sp2, n_l, n_den, n_th, n_ls, n_be, n_qk = [bump("x") for _ in range(9)]
            n_pack, n_o = bump("x"), bump("x")
            e_done, ln_done, squared = 1, 2, 14

            def pe(pe, mm):
                pe.wait_ge(s_y, n_y)
                proj_pe(pe, mm, m["p1"], lambda i: lambda k: Y[:, k, 0:S])
                idx = m["la"]
                pe.wait_ge(s_gw, 80)
                pe.wait_ge(s_ev, idx)
                for h in range(4):
                    pe.wait_ge(s_ev, idx - 3)
                    mm(PS[idx % 4][:, 0:S], WA2[0:16, h * P:(h + 1) * P], ZA[0:16], start=True, stop=True)\
                        .then_inc(s_mm, 1)
                    idx += 1
                pe.wait_ge(s_xr, n_xc)
                for f in range(DT):
                    for g in range(2):
                        pe.wait_ge(s_ev, idx - 3)
                        for b in range(2):
                            h = slice(b * HD, (b + 1) * HD)
                            last = mm(PS[idx % 4][h, 0:S], RGW[h, g, f], XC[h, f], start=True, stop=True)
                        last.then_inc(s_mm, 1)
                        idx += 1
                sec = m["pv"]
                idx = sec["t0"]
                for j in range(4):
                    c = sec["w0"] + j
                    pe.wait_ge(s_w[c % 2], 32 * (c // 2 + 1))
                    for tt in range(2):
                        pe.wait_ge(s_ev, idx - 3)
                        for k in range(DT):
                            last = mm(PS[idx % 4][:, 0:S], Y[:, k, tt * P:(tt + 1) * P], wide(c, DT)[:, k, :],
                                      start=(k == 0), stop=(k == DT - 1))
                        last.then_inc(s_mm, 1)
                        idx += 1
                proj_pe(pe, mm, m["p2"], lambda i: lambda k: Y[:, k, 0:S])
                idx = m["sc"]
                pe.wait_ge(s_ev, idx)
                pe.wait_ge(s_xr, n_qk)
                for h in range(4):
                    for c in range(4):
                        tok = slice(c * HD, (c + 1) * HD)
                        a = (h * 2 + c // 2) * HD
                        last = mm(PS[idx % 4][(c % 2) * HD:(c % 2 + 1) * HD, a:a + HD], KI[:, h, tok], QD[:, h, tok],
                                  start=True, stop=True)
                last.then_inc(s_mm, 1)
                idx += 1
                for tt in range(2):
                    for h in range(4):
                        last = nc.tensor.transpose(PS[idx % 4][:, h * P:(h + 1) * P], KE[:, h, tt * P:(tt + 1) * P],
                                                   ident)
                    last.then_inc(s_mm, 1)
                    idx += 1
                pe.wait_ge(s_ev, idx)
                for h in range(4):
                    for par in range(2):
                        pe.wait_ge(s_ev, idx - 3)
                        r = slice(par * HD, (par + 1) * HD)
                        for tt in range(2 - par):
                            last = mm(PS[idx % 4][:, tt * S:(tt + 1) * S], KET[r, tt, h * P:(h + 1) * P],
                                      VTOK[r, tt, h * S:(h + 1) * S], start=True, stop=True)
                        last.then_inc(s_mm, 1)
                        idx += 1
                pe.wait_ge(s_ev, idx)
                for h in range(4):
                    for q in range(2):
                        pe.wait_ge(s_ev, idx - 3)
                        v = slice(h * S + q * P, h * S + (q + 1) * P)
                        for c in range(4):
                            o = PS[idx % 4][:, c * HD:(c + 1) * HD]
                            last = mm(o, VTOK[:, c // 2, v], SCO[:, h, c], start=True, stop=(c == 0))
                            if c:
                                last = mm(o, ST[:, h, c - 1, q * P:(q + 1) * P], QD[:, h, c * HD:(c + 1) * HD],
                                          start=False, stop=True)
                        last.then_inc(s_mm, 1)
                        idx += 1
                pe.wait_ge(s_ga, squared)
                for g in range(2):
                    for u in range(2):
                        h = 2 * g + u
                        for q in range(2):
                            last = mm(PS[idx % 4][:, u * S:(u + 1) * S], ones, AI[:, 2 * h + q], start=(q == 0),
                                      stop=(q == 1))
                    last.then_inc(s_mm, 1)
                    idx += 1
                pe.wait_ge(s_ev, idx)
                pe.wait_ge(s_xr, n_o)
                proj_pe(pe, mm, m["pout"], lambda i: lambda k: Z16[:, k])

            def act(act, A, link):
                act.wait_ge(s_xr, n_sp)
                A(SPL[:, 1], SPL[:, 0], ACT.Exp, scale=-1.0).then_inc(s_ga, 1)
                act.wait_ge(s_ga, e_done)
                A(SPL[:, 2], SPL[:, 1], ACT.Ln, bias=eps["one"]).then_inc(s_ga, 1)
                idx = m["p1"]["t0"]
                for i in range(17):
                    act.wait_ge(s_mm, idx + 1)
                    b = PS[idx % 4][:, 0:S]
                    if i < 8:
                        A(XAP[:, i, 3:S + 3], b, ACT.Copy).then_inc(s_ev, 1)
                    elif i == 8:
                        A(ZA[0:16], b[0:16], ACT.Copy).then_inc(s_ev, 1)
                    elif i < 13:
                        A(QG[:, i - 9], b, ACT.Copy, scale=P ** -0.5).then_inc(s_ev, 1)
                    else:
                        A(KG[:, i - 13], b, ACT.Copy).then_inc(s_ev, 1)
                    idx += 1
                for h in range(4):
                    act.wait_ge(s_mm, idx + 1)
                    A(LA[:, h], PS[idx % 4][:, 0:S], ACT.Identity, bias=vec("gla_ba_2", h)).then_inc(s_ev, 1)
                    idx += 1
                for f in range(DT):
                    for g, (dst, name) in enumerate(((AR_, "rg_ba_2"), (AI, "rg_bx_2"))):
                        act.wait_ge(s_mm, idx + 1)
                        A(dst[:, f], PS[idx % 4][:, 0:S], ACT.Sigmoid, bias=vec(name, f)).then_inc(s_ev, 1)
                        idx += 1
                for i in range(24):
                    act.wait_ge(s_mm, idx + 1)
                    b = PS[idx % 4][:, 0:S]
                    if i < 8:
                        j, tt = i // 2, i % 2
                        A(VTOK[:, tt, j * S:(j + 1) * S], b, ACT.Copy).then_inc(s_ev, 1)
                    elif i < 16:
                        A(Z16[:, i], b, ACT.Silu).then_inc(s_ev, 1)
                    else:
                        A(Z16[:, i - 16], b, ACT.Gelu_apprx_tanh).then_inc(s_ev, 1)
                    idx += 1
                    if i == 0:
                        act.wait_ge(s_ev, m["rg"] + 16)
                        A(DX, LA, ACT.Abs).then_inc(s_ga, 1)
                        act.wait_ge(s_ga, 3)
                        A(DX, DX, ACT.Exp, scale=-1.0).then_inc(s_ga, 1)
                        act.wait_ge(s_ga, 4)
                        A(DX, DX, ACT.Ln, bias=eps["one"]).then_inc(s_ga, 1)
                    elif i == 2:
                        act.wait_ge(s_xr, n_l)
                        A(TH, AR_, ACT.Tanh, scale=-1.0).then_inc(s_ga, 1)
                        act.wait_ge(s_ga, 6)
                        A(AR_, AR_, ACT.Exp).then_inc(s_ga, 1)
                    elif i == 6:
                        act.wait_ge(s_xr, n_th)
                        A(TH, TH, ACT.Sqrt).then_inc(s_ga, 1)
                    elif i == 7:
                        act.wait_ge(s_xr, n_be)
                        A(QD, BC, ACT.Exp)
                        A(KI, BC, ACT.Exp, scale=-1.0)
                        A(KE, DX, ACT.Exp).then_inc(s_ga, 1)
                        bc = BC.rearrange("p h (c e) -> p h c e", c=4)
                        A(DEC[:, :, :], bc[:, :, :, HD - 1], ACT.Exp).then_inc(s_ga, 1)
                act.wait_ge(s_ev, m["sq"])
                A(AI, AR_, ACT.Square).then_inc(s_ga, squared - 10)
                idx = m["sq"]
                for g in range(2):
                    act.wait_ge(s_mm, idx + 1)
                    A(RR[:, 2 * g:2 * g + 2], PS[idx % 4][:, :].rearrange("p (a b) -> p a b", a=2), ACT.Sqrt,
                      bias=eps["rms2"], scale=1.0 / S).then_inc(s_ev, 1)
                    idx += 1

            def dve(dve, V, link):
                def say(ins, k):
                    ins.then_inc(s_xr, 1)
                    dve.wait_ge(s_xr, k)

                lam = vec("rg_lam_2", 0, DT)
                link(V.memset(XAP[:, :, 0:3], 0.0))
                say(V.scalar_tensor_tensor(SPL[:, 0], lam, -1.0, lam, ALU.mult, ALU.max), n_sp)
                dve.wait_ge(s_ga, ln_done)
                link(V.tensor_scalar(SPL[:, 3], SPL[:, 1], 1.0, -1.0, ALU.add, ALU.add))
                link(V.tensor_scalar(SPL[:, 3], SPL[:, 3], 1e-30, None, ALU.max))
                link(V.reciprocal(SPL[:, 3], SPL[:, 3]))
                link(V.tensor_tensor(SPL[:, 1], SPL[:, 1], SPL[:, 3], ALU.mult))
                link(V.tensor_tensor(SPL[:, 1], SPL[:, 1], SPL[:, 2], ALU.mult))
                link(V.tensor_scalar(SPL[:, 3], lam, -1.0, 0.0, ALU.mult, ALU.max))
                link(V.tensor_tensor(SPL[:, 1], SPL[:, 1], SPL[:, 3], ALU.add))
                link(V.tensor_scalar(SPL[:, 4], SPL[:, 1], -8.0, None, ALU.mult))
                dve.wait_ge(s_ev, m["p1"]["t0"] + 8)
                for f in range(DT):
                    ins = V.tensor_scalar(XC[:, f], XAP[:, f, 0:S], vec("conv_w_2", f), vec("conv_b_2", f), ALU.mult,
                                          ALU.add)
                for k in range(1, 4):
                    link(ins)
                    for f in range(DT):
                        ins = V.scalar_tensor_tensor(XC[:, f], XAP[:, f, k:k + S], vec("conv_w_2", DT * k + f), XC[:, f],
                                                     ALU.mult, ALU.add)
                say(ins, n_xc)
                dve.wait_ge(s_ev, m["rg"] + 16)
                for f in range(DT):
                    ins = V.tensor_scalar(AR_[:, f], AR_[:, f], SPL[:, 4, f:f + 1], None, ALU.mult)
                say(ins, n_sp2)
                say(V.tensor_tensor(AI, AI, XC, ALU.mult), n_l)
                dve.wait_ge(s_ga, 5)
                link(V.tensor_scalar(LA, LA, 0.0, None, ALU.min))
                link(V.tensor_tensor(LA, LA, DX, ALU.subtract))
                say(V.tensor_scalar(LA, LA, 1.0 / 16.0, None, ALU.mult), n_den)
                dve.wait_ge(s_ga, 6)
                link(V.tensor_scalar(YH, TH, 1.0, None, ALU.add))
                link(V.reciprocal(YH, YH))
                say(V.scalar_tensor_tensor(TH, TH, 2.0, YH, ALU.mult, ALU.mult), n_th)
                for h in range(4):
                    ins = V.tensor_tensor_scan(BC[:, h], tab("reset"), LA[:, h], 0.0, ALU.mult, ALU.add)
                say(ins, n_ls)
                for h in range(4):
                    bc = BC[:, h].rearrange("p (c e) -> p c e", c=4)
                    ins = V.tensor_tensor(DX[:, h].rearrange("p (c e) -> p c e", c=4),
                                          bc[:, :, HD - 1:HD].to_broadcast([P, 4, HD]), bc, ALU.subtract)
                say(ins, n_be)
                dve.wait_ge(s_ga, 8)
                link(V.tensor_tensor(AI, AI, TH, ALU.mult))
                for f in range(DT):
                    ins = V.tensor_tensor_scan(XC[:, f], AR_[:, f], AI[:, f], 0.0, ALU.mult, ALU.add)
                link(ins)
                dve.wait_ge(s_ga, 10)
                V.tensor_tensor(QD, QD, QG, ALU.mult)
                V.tensor_tensor(KI, KI, KG, ALU.mult)
                say(V.tensor_tensor(KE, KE, KG, ALU.mult), n_qk)
                dve.wait_ge(s_ev, m["sc"])
                link(V.tensor_tensor(Z16[:, 0:DT], Z16[:, 0:DT], XC, ALU.mult))
                link(V.memset(SCO, 0.0))
                idx = m["sc"]
                dve.wait_ge(s_mm, idx + 1)
                pv = PS[idx % 4][:, :].rearrange("p (h c e) -> p h c e", h=4, c=2)
                sv = SCO.rearrange("p h (c two) e -> p h c two e", two=2)
                for par in range(2):
                    r = slice(par * HD, (par + 1) * HD)
                    for h in range(4):
                        ins = V.scalar_tensor_tensor(sv[r, h, :, par], pv[r, h], 3.0e38,
                                                     tab("incl0")[r].unsqueeze(1).to_broadcast([HD, 2, HD]), ALU.min,
                                                     ALU.mult)
                ins.then_inc(s_ev, 1)
                idx += 1
                for tt in range(2):
                    dve.wait_ge(s_mm, idx + 1)
                    V.tensor_copy(KET[:, tt], PS[idx % 4][:, :]).then_inc(s_ev, 1)
                    idx += 1
                for h in range(4):
                    dve.wait_ge(s_mm, idx + 2)
                    even, odd = PS[idx % 4], PS[(idx + 1) % 4]
                    link(V.tensor_copy(ST[:, h, 0], even[:, 0:S]))
                    link(V.scalar_tensor_tensor(ST[:, h, 1], ST[:, h, 0], DEC[:, h, 1:2], odd[:, 0:S], ALU.mult,
                                                ALU.add))
                    V.scalar_tensor_tensor(ST[:, h, 2], ST[:, h, 1], DEC[:, h, 2:3], even[:, S:2 * S], ALU.mult,
                                           ALU.add).then_inc(s_ev, 2)
                    idx += 2
                for i in range(DT):
                    dve.wait_ge(s_mm, idx + 1)
                    V.tensor_copy(AR_[:, i], PS[idx % 4][:, 0:S]).then_inc(s_ev, 1)
                    idx += 1
                dve.wait_ge(s_ev, m["sq"] + 2)
                link(V.reciprocal(RR, RR))
                o4 = AR_.rearrange("p (h q) t -> p h q t", q=2)
                for q in range(2):
                    ins = V.tensor_tensor(o4[:, :, q], o4[:, :, q], RR, ALU.mult)
                say(ins, n_pack)
                for i in range(DT):
                    ins = V.scalar_tensor_tensor(Z16[:, 8 + i], AR_[:, i], vec("gla_norm_g_2", i % 2), Z16[:, 8 + i],
                                                 ALU.mult, ALU.mult)
                say(ins, n_o)
                proj_add(dve, V, m["pout"])

            add("do", pe, act, dve)

        NH = 8
        CQ = region(0, [3, S])
        QN = region(768, [NH, S])
        KN = region(2816, [NH, S])
        QP = region(4864, [NH, S])
        QR = region(6912, [NH, S])
        KP = region(8960, [S])
        KPR = region(9216, [S])
        COS, SIN = region(9472, [S]), region(9728, [S])
        ANG = region(9984, [3, S])
        VM = region(10752, [2, NH * P])
        ZM = region(12800, [NH, S])
        SCR = spare(512, 2, 2, S)
        PEX = spare(1536, 2, 2, S)
        PTR = spare(2560, 2, 2, S)
        SQM = spare(3584, 3, S)
        MXS = sb("MXS", [P, 2, 6])
        POSI = sb("POSI", [HD, S], I32)
        s_pos = sem("positions_loaded")
        s_ma = sem("mla_scalar_step")
        s_mp = sem("softmax_max_ready")
        s_me = sem("softmax_exp_ready")
        s_mn = sem("softmax_scaled")
        s_mt = sem("probabilities_copied")

        def mla_plan():
            w = t["odd_w_in_2"][0].rearrange("(k p) n -> p k n", p=P)
            m = dict(p1=proj([(w[:, :, 0:256], [0, 1]), (w[:, :, 256:448], [0, 1])]))
            m["nrm"] = count["t"]
            count["t"] += 2
            m["up"] = proj([(t["w_q_up_2"][0].rearrange("(k p) n -> p k n", p=P), list(range(16))),
                            (t["w_kv_up_2"][0].rearrange("(k p) n -> p k n", p=P), list(range(12)))])
            m["rot"] = count["t"]
            m["att"] = m["rot"] + 5
            count["t"] = m["att"] + 3 * NH
            wo = t["odd_w_out_2"][0].rearrange("(k p) n -> p k n", p=P)
            m["pout"] = proj([(wo[:, :, 256 * j:256 * (j + 1)], [0, 1]) for j in range(4)])
            m["t1"] = count["t"]

            def first(sp):
                sp.dma_start(POSI[:, :], t["positions_2"][0:1, :].to_broadcast([HD, S])).then_inc(s_pos, 16)

            m["p1"]["first"] = first
            m["phases"] = mla_phases
            return m

        def mla_phases(layer):
            m = mixers["mla"]
            n_y = n["y"]
            n_ang, n_lat, n_rope = [bump("x") for _ in range(3)]

            def pe(pe, mm):
                pe.wait_ge(s_y, n_y)
                proj_pe(pe, mm, m["p1"], lambda i: lambda k: Y[:, k, 0:S])
                idx = m["nrm"]
                pe.wait_ge(s_ma, 1)
                pe.wait_ge(s_ev, idx)
                for g, tiles in enumerate(((0, 1), (2,))):
                    for q in tiles:
                        last = mm(PS[idx % 4][:, 0:S], ones, SQM[:, q], start=(q == tiles[0]), stop=(q == tiles[-1]))
                    last.then_inc(s_mm, 1)
                    idx += 1
                pe.wait_ge(s_xr, n_lat)
                sec = m["up"]
                c = sec["w0"]
                pe.wait_ge(s_w[c % 2], 32 * (c // 2 + 1))
                wq = wide(c, 2, 1536)
                idx = sec["t0"]
                pe.wait_ge(s_ev, idx)
                for part, (off, m_) in enumerate(((0, P), (P, HD))):
                    for h in range(NH):
                        pe.wait_ge(s_ev, idx - 3)
                        for k in range(2):
                            last = mm(PS[idx % 4][0:m_, 0:S], wq[:, k, 192 * h + off:192 * h + off + m_], CQ[:, k],
                                      start=(k == 0), stop=(k == 1))
                        last.then_inc(s_mm, 1)
                        idx += 1
                c += 1
                pe.wait_ge(s_w[c % 2], 32 * (c // 2 + 1))
                wk = wide(c, 1, 2048)[:, 0].rearrange("p (h two n) -> p h two n", h=NH, two=2)
                for h in range(NH):
                    pe.wait_ge(s_ev, idx - 3)
                    mm(PS[idx % 4][:, 0:S], wk[:, h, 0], CQ[:, 2], start=True, stop=True).then_inc(s_mm, 1)
                    idx += 1
                for tt in range(2):
                    for g in range(2):
                        pe.wait_ge(s_ev, idx - 3)
                        mm(PS[idx % 4][:, :].rearrange("p (h n) -> p h n", h=4), CQ[:, 2, tt * P:(tt + 1) * P],
                           wk[:, 4 * g:4 * g + 4, 1], start=True, stop=True).then_inc(s_mm, 1)
                        idx += 1
                pe.wait_ge(s_ev, idx)
                for g in range(4):
                    pe.wait_ge(s_ev, idx - 3)
                    mm(PS[idx % 4][0:HD, :], tab("rot")[0:HD], QP[0:HD, 2 * g:2 * g + 2], start=True, stop=True)\
                        .then_inc(s_mm, 1)
                    idx += 1
                pe.wait_ge(s_ev, idx - 3)
                mm(PS[idx % 4][0:HD, 0:S], tab("rot")[0:HD], KP[0:HD], start=True, stop=True).then_inc(s_mm, 1)
                idx += 1
                pe.wait_ge(s_xr, n_rope)
                pe.wait_ge(s_ev, idx)

                def scores(h):
                    o = idx0 + 3 * h
                    bank = PS[h % 2]
                    for qt in range(2):
                        q = slice(qt * P, (qt + 1) * P)
                        mm(bank[:, qt * S:(qt + 1) * S], QN[:, h, q], KN[:, h], start=True, stop=False)
                        last = mm(bank[:, qt * S:(qt + 1) * S], QP[0:HD, h, q], KP[0:HD], start=False, stop=True)
                    last.then_inc(s_mm, 1)

                idx0 = idx

                def values(h):
                    pe.wait_ge(s_mn, h + 1)
                    for kt in range(2):
                        for qt in range(2):
                            last = nc.tensor.transpose(PS[2][:, kt * S + qt * P:kt * S + (qt + 1) * P],
                                                       PEX[:, h % 2, qt, kt * P:(kt + 1) * P], ident)
                    last.then_inc(s_mm, 1)
                    pe.wait_ge(s_mt, h + 1)
                    for kt in range(2):
                        last = mm(PS[3][:, 0:S], VM[:, kt, h * P:(h + 1) * P], PTR[:, h % 2, kt], start=(kt == 0),
                                  stop=(kt == 1))
                    last.then_inc(s_mm, 1)

                scores(0)
                for h in range(NH):
                    if h + 1 < NH:
                        if h >= 1:
                            pe.wait_ge(s_mp, 2 * h)
                        scores(h + 1)
                    if h:
                        pe.wait_ge(s_ev, idx0 + 3 * h)
                    values(h)
                pe.wait_ge(s_ev, m["pout"]["t0"])
                proj_pe(pe, mm, m["pout"], lambda i: lambda k: ZM[:, k])

            def act(act, A, link):
                idx = m["p1"]["t0"]
                for i in range(4):
                    act.wait_ge(s_mm, idx + 1)
                    if i < 3:
                        A(CQ[:, i], PS[idx % 4][:, 0:S], ACT.Copy).then_inc(s_ev, 1)
                    else:
                        A(KP[0:HD], PS[idx % 4][0:HD, 0:S], ACT.Copy).then_inc(s_ev, 1)
                    idx += 1
                act.wait_ge(s_ev, idx)
                A(SQM, CQ, ACT.Square).then_inc(s_ma, 1)
                for g in range(2):
                    act.wait_ge(s_mm, idx + 1)
                    A(ANG[:, g], PS[idx % 4][:, 0:S], ACT.Sqrt, bias=eps["rms2"], scale=1.0 / (256, 128)[g])\
                        .then_inc(s_ev, 1)
                    idx += 1
                for i in range(16):
                    act.wait_ge(s_mm, idx + 1)
                    if i < 8:
                        A(QN[:, i], PS[idx % 4][:, 0:S], ACT.Copy, scale=192 ** -0.5).then_inc(s_ev, 1)
                    else:
                        A(QP[0:HD, i - 8], PS[idx % 4][0:HD, 0:S], ACT.Copy, scale=192 ** -0.5).then_inc(s_ev, 1)
                    idx += 1
                for i in range(12):
                    act.wait_ge(s_mm, idx + 1)
                    if i < 8:
                        A(KN[:, i], PS[idx % 4][:, 0:S], ACT.Copy).then_inc(s_ev, 1)
                    else:
                        i -= 8
                        A(VM[:, i // 2, (i % 2) * 512:(i % 2 + 1) * 512], PS[idx % 4][:, :], ACT.Copy)\
                            .then_inc(s_ev, 1)
                    idx += 1
                act.wait_ge(s_xr, n_ang)
                A(COS[0:HD], COS[0:HD], ACT.Sin)
                A(SIN[0:HD], SIN[0:HD], ACT.Sin).then_inc(s_ma, 1)
                for h in range(NH):
                    for qt in range(2):
                        act.wait_ge(s_mp, 2 * h + qt + 1)
                        if h >= 2:
                            act.wait_ge(s_ev, m["att"] + 3 * (h - 1))
                        A(PEX[:, h % 2, qt], SCR[:, h % 2, qt], ACT.Exp, bias=MXS[:, h % 2, qt:qt + 1],
                          accum_out=MXS[:, h % 2, 2 + qt:3 + qt]).then_inc(s_me, 1)

            def dve(dve, V, link):
                def say(ins, k):
                    ins.then_inc(s_xr, 1)
                    dve.wait_ge(s_xr, k)

                dve.wait_ge(s_pos, 16)
                h64 = slice(0, HD)
                link(V.tensor_copy(SIN[h64], POSI[:, :]))
                link(V.tensor_scalar(SIN[h64], SIN[h64], tab("freq")[h64], None, ALU.mult))
                link(V.tensor_scalar(COS[h64], SIN[h64], 1.0 / TWO_PI, 12582912.0, ALU.mult, ALU.add))
                link(V.tensor_scalar(COS[h64], COS[h64], -12582912.0, None, ALU.add))
                link(V.scalar_tensor_tensor(SIN[h64], COS[h64], -6.28125, SIN[h64], ALU.mult, ALU.add))
                link(V.scalar_tensor_tensor(SIN[h64], COS[h64], -(TWO_PI - 6.28125), SIN[h64], ALU.mult, ALU.add))
                link(V.tensor_scalar(COS[h64], SIN[h64], np.pi / 2, None, ALU.add))
                link(V.tensor_scalar(ANG[h64, 2], COS[h64], np.pi, -TWO_PI, ALU.is_gt, ALU.mult))
                link(V.tensor_tensor(COS[h64], COS[h64], ANG[h64, 2], ALU.add))
                link(V.tensor_scalar(COS[h64], COS[h64], 3.1415925, -3.1415925, ALU.min, ALU.max))
                say(V.tensor_scalar(SIN[h64], SIN[h64], 3.1415925, -3.1415925, ALU.min, ALU.max), n_ang)
                dve.wait_ge(s_ev, m["up"]["t0"])
                link(V.reciprocal(ANG[:, 0:2], ANG[:, 0:2]))
                for i in range(3):
                    g = vec("q_norm_g_2", i) if i < 2 else vec("kv_norm_g_2", 0)
                    ins = V.scalar_tensor_tensor(CQ[:, i], CQ[:, i], g, ANG[:, i // 2], ALU.mult, ALU.mult)
                say(ins, n_lat)
                dve.wait_ge(s_ma, 2)
                idx = m["rot"]
                for g in range(4):
                    dve.wait_ge(s_mm, idx + 1)
                    V.tensor_tensor(QR[h64, 2 * g:2 * g + 2], PS[idx % 4][h64, :].rearrange("p (a b) -> p a b", a=2),
                                    SIN[h64].unsqueeze(1).to_broadcast([HD, 2, S]), ALU.mult).then_inc(s_ev, 1)
                    idx += 1
                dve.wait_ge(s_mm, idx + 1)
                V.tensor_tensor(KPR[h64], PS[idx % 4][h64, 0:S], SIN[h64], ALU.mult).then_inc(s_ev, 1)
                idx += 1
                dve.wait_ge(s_ev, idx)
                link(V.tensor_tensor(QP[h64], QP[h64], COS[h64].unsqueeze(1).to_broadcast([HD, NH, S]), ALU.mult))
                link(V.tensor_tensor(QP[h64], QP[h64], QR[h64], ALU.add))
                link(V.tensor_tensor(KP[h64], KP[h64], COS[h64], ALU.mult))
                say(V.tensor_tensor(KP[h64], KP[h64], KPR[h64], ALU.add), n_rope)

                def soft(h):
                    dve.wait_ge(s_mm, idx + (1 if h == 0 else 3 * h - 1))
                    for qt in range(2):
                        if h >= 2:
                            dve.wait_ge(s_me, 2 * (h - 2) + qt + 1)
                        link(V.tensor_tensor(SCR[:, h % 2, qt], PS[h % 2][:, qt * S:(qt + 1) * S], tab("causal")[:, qt * S:(qt + 1) * S], ALU.add))
                        V.tensor_reduce(MXS[:, h % 2, qt:qt + 1], SCR[:, h % 2, qt], AX.X, ALU.max, negate=True)\
                            .then_inc(s_mp, 1)
                        dve.wait_ge(s_mp, 2 * h + qt + 1)

                def rest(h):
                    dve.wait_ge(s_me, 2 * h + 2)
                    link(V.reciprocal(MXS[:, h % 2, 4:6], MXS[:, h % 2, 2:4]))
                    for qt in range(2):
                        ins = V.tensor_scalar(PEX[:, h % 2, qt], PEX[:, h % 2, qt], MXS[:, h % 2, 4 + qt:5 + qt], None,
                                              ALU.mult)
                    ins.then_inc(s_mn, 1)

                def out_(h):
                    seen = idx + 1 + 3 * h + (1 if h + 1 < NH else 0)
                    dve.wait_ge(s_mm, seen + 1)
                    V.tensor_copy(PTR[:, h % 2], PS[2][:, :].rearrange("p (a b) -> p a b", a=2)).then_inc(s_mt, 1)
                    dve.wait_ge(s_mm, seen + 2)
                    V.tensor_copy(ZM[:, h], PS[3][:, 0:S]).then_inc(s_ev, 3)
                    dve.wait_ge(s_ev, idx + 3 * (h + 1))

                soft(0)
                for h in range(NH):
                    rest(h)
                    if h + 1 < NH:
                        soft(h + 1)
                    out_(h)
                proj_add(dve, V, m["pout"])

            add("do", pe, act, dve)

        mixers = {}
        F = [ffn(f1[0], d1[0], 2 * S, (0, 4, 14), 0, 2, 0.5)]
        mixers["rwkv"] = rwkv_plan()
        F += [ffn(f2[0], d2[0], S, (1, 0, 18), 0, 8, 0.5),
              ffn(f1[1], d1[1], S, (2, 0, 18), 1, 2, 0.5)]
        mixers["conv"] = conv_plan()
        F += [ffn(f2[1], d2[1], S, (3, 0, 18), 1, 8, 0.5),
              ffn(fi[0, 0], fo[0, 0], S, None, 2, 2, 0.5)]
        mixers["gla"] = gla_plan()
        F += [ffn(fi[0, 1], fo[0, 1], S, None, 2, 8, 0.5),
              ffn(fi[1, 0], fo[1, 0], S, None, 3, 2, 0.5)]
        mixers["mla"] = mla_plan()
        F += [ffn(fi[1, 1], fo[1, 1], S, None, 3, 8, 0.5)]
        ends = [e for sec in plan for e in sec["ends"]]

        phases = []
        n = dict(sq=0, ns=0, rs=0, y=0, x=0, mod=1)

        def add(kind, *args):
            phases.append((kind, *args))

        def bump(name):
            n[name] += PIECES if name == "y" else 1
            return n[name]

        def sum_squares(T, scale, e, centred=False):
            seqs = T // S
            for i in range(PIECES):
                ks = slice(DT // PIECES * i, DT // PIECES * (i + 1))
                add("squares", [X[:, s, ks] for s in range(seqs)], [SQ[:, ks, s * S:(s + 1) * S] for s in range(seqs)],
                    x_waits(ks.stop, n["x"] - PIECES + 1 + i if centred else None))
            add("sum", T, SQ, DT, [bump("sq") for i in range(PIECES)], n["rs"])
            add("root", T, scale, e, bump("ns"), n["y"], n["x"])
            return bump("rs")

        def x_waits(k=DT, n_x=None):
            done = done_t[0] - (DT - k) if done_t[0] > VEC_TILES else VEC_TILES
            n_x = n["x"] if n_x is None else n_x
            return [(s_xc, 2 * DT), (s_ev, done)] + ([(s_xr, n_x)] if n_x else [])

        done_t = [VEC_TILES]

        def norm(layer, k, T):
            n_rs = sum_squares(T, 1.0 / D, "rms")
            add("rms", layer, 3 * k, T, n_rs, vec("norm_g", 24 * layer + 8 * k, 8), bump("y"))

        def feed(i, layer, k, w):
            if i:
                add("gates", layer, 3 * k + 2, w, F[i]["T"] > S)
            add("ffn", i, n["y"])
            done_t[0] = F[i]["t1"]

        def deepnorm(at, then):
            add("xsum", [x_waits(k + 1) for k in range(DT)], n["rs"], bump("ns"))
            n["x"] += PIECES
            add("center", n["ns"], n["x"])
            n_rs = sum_squares(S, 1.0 / D, "ln", centred=True)
            add("layer_norm", n_rs, at, bump("x"), then, bump("y") if then else None)

        def mixer(name, layer):
            if name in mixers:
                add("gates", layer, 5, 1.0, False)
                if "phases" in mixers[name]:
                    mixers[name]["phases"](layer)
                else:
                    add("mix", name, n["y"])
                done_t[0] = mixers[name]["t1"]

        def program():
            norm(0, 0, 2 * S)
            feed(0, 0, 0, 0.5)
            bump("mod")
            norm(0, 1, 2 * S)
            mixer("rwkv", 0)
            if stop == 1:
                return
            norm(0, 2, S)
            feed(1, 0, 2, 0.5)
            add("mods", 1, 0, 18, bump("mod"))
            norm(1, 0, S)
            feed(2, 1, 0, 0.5)
            add("mods", 2, 0, 18, bump("mod"))
            norm(1, 1, S)
            mixer("conv", 1)
            norm(1, 2, S)
            feed(3, 1, 2, 0.5)
            add("mods", 3, 0, 18, bump("mod"))
            n_rs = sum_squares(S, 1.0 / D, "rms")
            add("scaled", n_rs, vec("final_g", 0, 8), bump("x"))
            if stop == 2:
                return
            for layer in (2, 3):
                at = 24 * (layer - 2)
                if layer == 2:
                    add("modulate", layer, 0, bump("y"))
                feed(2 * layer, layer, 0, 0.5)
                deepnorm(at, (layer, 3))
                mixer("gla" if layer == 2 else "mla", layer)
                deepnorm(at + 8, (layer, 6))
                feed(2 * layer + 1, layer, 2, 0.5)
                deepnorm(at + 16, (3, 0) if layer == 2 else None)

        program()
        last_chunk = mixers["rwkv"]["pc"]["w0"] if stop == 1 else F[3]["w0"] if stop == 2 else 10 ** 6
        n_final = n["x"]

        block = ctx.enter_context(nc.Block())

        @block.sync
        def _(sp):
            sp.dma_start(CT[:], t["table"][:, 0:ncols]).then_inc(s_tab, 16)
            for s, name in ((0, "x"), (1, "ctx")):
                for h in range(2):
                    sp.dma_start(Y[:, :, :].rearrange("p a b -> p (a b)")[:, (2 * s + h) * D:(2 * s + h + 1) * D],
                                 t[name][0, h * P:(h + 1) * P, :]).then_inc(s_x, 16)

            def free(c):
                if c >= 2:
                    sp.wait_ge(s_mm, ends[c - 2])

            def load_gu(sec, j, u):
                c = sec["w0"] + u
                for g in range(2):
                    sp.dma_start(gate_up(c)[:, g], sec["gu"][:, :, bass.ds(j * (2 * P) + g * FF, 2 * P)])\
                      .then_inc(s_w[c % 2], 16)

            def load_down(sec, j, u):
                c = sec["w0"] + PAIRS + u
                for g in range(2):
                    ks = slice(g * PAIRS, (g + 1) * PAIRS)
                    sp.dma_start(wide(c, FT)[:, ks], sec["down"][:, ks, bass.ds(j * (2 * P), 2 * P)])\
                      .then_inc(s_w[c % 2], 16)

            for sec in plan:
                if sec["w0"] > last_chunk:
                    continue
                if sec["kind"] == "ffn":
                    for j in range(2):
                        free(sec["w0"] + j)
                        load_gu(sec, j, j)
                    base, per = sec["t0"], sec["per"]
                    with steps(sp, 2, PAIRS - 1, 2) as j:
                        for u in range(2):
                            sp.wait_ge(s_mm, j * per + (base + per * (u - 1)))
                            load_gu(sec, j + u, u)
                    free(sec["w0"] + PAIRS - 1)
                    load_gu(sec, PAIRS - 1, PAIRS - 1)
                    for j in range(4):
                        free(sec["w0"] + PAIRS + j)
                        load_down(sec, j, j)
                else:
                    if "first" in sec:
                        sec["first"](sp)
                    for j, (src, tiles) in enumerate(sec["chunks"]):
                        c = sec["w0"] + j
                        free(c)
                        kt, n = src.shape[1], src.shape[2]
                        ns = slice(0, n)
                        halves = [(slice(0, kt // 2), ns), (slice(kt // 2, kt), ns)] if kt > 1 else \
                            [(slice(0, 1), slice(0, n // 2)), (slice(0, 1), slice(n // 2, n))]
                        for ks, cs in halves:
                            sp.dma_start(wide(c, kt, n)[:, ks, cs], src[:, ks, cs]).then_inc(s_w[c % 2], 16)
                    if "then" in sec:
                        sec["then"](sp)
            for h in range(2):
                sp.wait_ge(s_oc, 2 * (h + 1))
                sp.dma_start(out[h * P:(h + 1) * P, :], OUT[:, h]).then_inc(s_out, 16)
            sp.wait_ge(s_out, 32)

        @block.gpsimd
        def _(pool):
            for name, rows in VEC_LIST:
                src = t[name]
                r = src.rearrange(f"{' '.join('abcd'[:len(src.shape)])} -> ({' '.join('abcd'[:len(src.shape)])})")
                r = r.rearrange("(r c) -> r c", c=P)
                at, done = VEC_AT[name], 0
                while done < rows:
                    n = min(rows - done, P - (at + done) % P)
                    q = at + done
                    pool.dma_start(VROWS[q % P:q % P + n, q // P, :], r[done:done + n, :]).then_inc(s_vec, 16)
                    done += n
            for layer in range(1 if stop == 1 else 4):
                if layer == 1 and "rwkv" in mixers:
                    scan_over(pool, 1)
                for u in range(2):
                    if 18 * layer + u >= 2:
                        pool.wait_ge(s_acc, 18 * layer + u - 1)
                    pool.dma_start(ADAW[:, u], ada_src[layer][:, :, u * ADA_COLS:(u + 1) * ADA_COLS])\
                        .then_inc(s_adaw[u], 16)
                with steps(pool, 2, ADA_CHUNKS, 2) as c:
                    for u in range(2):
                        pool.wait_ge(s_acc, c + (18 * layer + u - 1))
                        pool.dma_start(ADAW[:, u], ada_src[layer][:, :, bass.ds((c + u) * ADA_COLS, ADA_COLS)])\
                            .then_inc(s_adaw[u], 16)

        @block.tensor
        def _(pe):
            mm = nc.tensor.matmul

            def wait_bank(idx, dyn=None):
                if dyn is not None:
                    pe.wait_ge(s_ev, dyn + (idx - 3))
                elif idx >= 4:
                    pe.wait_ge(s_ev, idx - 3)

            def columns(layer, c, dyn=None):
                a = 18 * layer + c
                pe.wait_ge(s_acc, a + 1 if dyn is None else dyn + (a + 1))
                seqs = 2 if layer == 0 else 1
                for s in range(seqs):
                    for q in range(4):
                        col = s * 128 + 4 * c + q if dyn is None else bass.ds(dyn * 4 + (s * 128 + 4 * c + q), 1)
                        o = ADA_PS[:, col:col + 1] if dyn is None else ADA_PS[:, col]
                        last = mm(o, ACC[:, a % 2, s, q * P:(q + 1) * P], ones[:, 0:1], start=True, stop=True)
                last.then_inc(s_col, 1)

            def ffn(sec, n_y):
                T, w0, t0, per = sec["T"], sec["w0"], sec["t0"], sec["per"]

                def unit(j, u, dyn, ada):
                    c = w0 + u
                    n_w = 32 * (c // 2 + 1)
                    pe.wait_ge(s_w[c % 2], n_w if dyn is None else dyn * 16 + n_w)
                    for q in range(2):
                        for g in range(2):
                            idx = t0 + per * u + (2 * q + g if per == 4 else q)
                            bank = PS[idx % 4]
                            if per == 4 or g == 0:
                                wait_bank(idx, None if dyn is None else dyn * per)
                            o = bank[:, :] if per == 4 else bank[:, g * S:(g + 1) * S]
                            for k in range(DT):
                                if u == 0 and q == 0 and g == 0 and k % (DT // PIECES) == 0:
                                    pe.wait_ge(s_y, n_y - PIECES + 1 + k // (DT // PIECES))
                                last = mm(o, gate_up(c)[:, g, k, q * P:(q + 1) * P], Y[:, k, 0:T],
                                          start=(k == 0), stop=(k == DT - 1))
                            if per == 4 or g == 1:
                                last.then_inc(s_mm, 1)
                    if ada:
                        layer, first, _ = sec["ada"]
                        for v in range(2):
                            columns(layer, first + 2 * u + v, None if dyn is None else dyn * 2)

                if sec["ada"] and sec["ada"][1] == 0:
                    pe.wait_ge(s_mod, sec["ada"][0] + 1)
                units_ada = sec["ada"][2] // 2 if sec["ada"] else 0
                pairs = units_ada // 2
                if pairs:
                    with steps(pe, 0, 2 * pairs, 2) as j:
                        for u in range(2):
                            unit(j, u, j, True)
                rest = 2 * pairs
                if units_ada % 2:
                    unit(rest, rest, None, True)
                    rest += 1
                more = (PAIRS - rest) // 2
                if more:
                    with steps(pe, 0, 2 * more, 2) as j:
                        for u in range(2):
                            unit(j, rest + u, j, False)
                    rest += 2 * more
                if rest < PAIRS:
                    unit(rest, rest, None, False)
                pe.wait_ge(s_ev, t0 + per * PAIRS)
                td = t0 + per * PAIRS
                with steps(pe, 0, 4, 2) as j:
                    for u in range(2):
                        c = w0 + PAIRS + u
                        pe.wait_ge(s_w[c % 2], j * 16 + 32 * (c // 2 + 1))
                        for q in range(2):
                            idx = td + 2 * u + q
                            wait_bank(idx, j * 2)
                            for k in range(FT):
                                last = mm(PS[idx % 4][:, 0:T], wide(c, FT)[:, k, q * P:(q + 1) * P], H[:, k, 0:T],
                                          start=(k == 0), stop=(k == FT - 1))
                            last.then_inc(s_mm, 1)

            def total(T, src, kt, n_sq, n_rs):
                if n_rs:
                    pe.wait_ge(s_rs, n_rs)
                for k in range(kt):
                    if k % (kt // len(n_sq)) == 0:
                        pe.wait_ge(s_sq, n_sq[k // (kt // len(n_sq))])
                    last = mm(NORM_PS[:, 0:T], ones, src[:, k, 0:T], start=(k == 0), stop=(k == kt - 1))
                last.then_inc(s_ns, 1)

            pe.wait_ge(s_tab, 16)
            pe.wait_ge(s_vec, 16 * VEC_LOADS)
            for v in range(VEC_TILES):
                rows = min(P, VEC_ROWS - v * P)
                nc.tensor.transpose(PS[v // 4][:, (v % 4) * P:(v % 4) * P + rows], VROWS[0:rows, v, :],
                                    ident[0:rows, 0:rows]).then_inc(s_mm, 1)
            pe.wait_ge(s_ev, VEC_TILES)
            for c in range(4):
                columns(0, c)
            pe.wait_ge(s_x, 64)
            for s in range(2):
                for k in range(DT):
                    if 8 * s + k >= 2:
                        pe.wait_ge(s_xc, 8 * s + k - 1)
                    for h in range(2):
                        src = Y[:, :, :].rearrange("p a b -> p (a b)")
                        src = src[:, (2 * s + h) * D + k * P:(2 * s + h) * D + (k + 1) * P]
                        last = nc.tensor.transpose(PS[6 + k % 2][:, h * P:(h + 1) * P], src, ident)
                    last.then_inc(s_xT, 1)
            for ph in phases:
                if ph[0] == "ffn":
                    ffn(F[ph[1]], ph[2])
                elif ph[0] == "sum":
                    total(*ph[1:])
                elif ph[0] == "xsum":
                    pe.wait_ge(s_rs, ph[2])
                    for k in range(DT):
                        for q, v in ph[1][k]:
                            pe.wait_ge(q, v)
                        last = mm(NORM_PS[:, 0:S], ones, X[:, 0, k], start=(k == 0), stop=(k == DT - 1))
                    last.then_inc(s_ns, 1)
                elif ph[0] == "do":
                    if ph[1]:
                        ph[1](pe, mm)
                elif ph[0] == "mix":
                    mixers[ph[1]]["pe"](pe, mm, ph)
            if n_final:
                pe.wait_ge(s_xr, n_final)
            pe.wait_ge(s_ev, done_t[0])
            for h in range(2):
                for g in range(2):
                    if 2 * h + g >= 2:
                        pe.wait_ge(s_oc, 2 * h + g - 1)
                    for k in range(4):
                        last = nc.tensor.transpose(PS[g][:, k * P:(k + 1) * P], X[:, 0, 4 * g + k, h * P:(h + 1) * P],
                                                   ident)
                    last.then_inc(s_o, 1)

        @block.scalar
        def _(act):
            A = nc.scalar.activation
            link = Chain(act, s_act)

            def ffn(sec):
                T, t0, per, k0 = sec["T"], sec["t0"], sec["per"], sec["silu0"]

                def gate(f, u, dyn):
                    idx = t0 + (2 * u if per == 4 else u)
                    act.wait_ge(s_mm, idx + 1 if dyn is None else dyn * (per // 2) + (idx + 1))
                    back = t0 + (per // 2) * (u - 1)
                    if dyn is not None:
                        act.wait_ge(s_ev, dyn * (per // 2) + back)
                    elif back > 0:
                        act.wait_ge(s_ev, back)
                    bank = idx if dyn is None else idx + per
                    A(SIL[:, u % 2, 0:T], PS[bank % 4][:, 0:T], ACT.Silu).then_inc(s_silu, 1)

                gate(0, 0, None)
                gate(1, 1, None)
                with steps(act, 2, FT, 4) as f:
                    for u in range(4):
                        gate(f, u, f)

            def squares(src, dst, n_wait, kt=DT):
                for q, w in n_wait:
                    act.wait_ge(q, w)
                for i, (o, s_) in enumerate(zip(dst, src)):
                    last = A(o, s_, ACT.Square)
                last.then_inc(s_sq, 1)

            def root(T, scale, e, n, n_y, n_x):
                act.wait_ge(s_ns, n)
                if n_y:
                    act.wait_ge(s_y, n_y)
                if n_x:
                    act.wait_ge(s_xr, n_x)
                A(RS[:, 0:T], NORM_PS[:, 0:T], ACT.Sqrt, bias=eps[e], scale=scale).then_inc(s_rs, 1)

            act.wait_ge(s_ev, VEC_TILES)
            A(SC[:, 0, :], vec("c", 0, DT), ACT.Silu)
            A(SC[:, 1, :], vec("c_ctx", 0, DT), ACT.Silu)
            A(SC[:, 2, :], vec("c_2", 0, DT), ACT.Silu).then_inc(s_sc, 1)
            for ph in phases:
                if ph[0] == "ffn":
                    ffn(F[ph[1]])
                elif ph[0] == "squares":
                    squares(*ph[1:])
                elif ph[0] == "root":
                    root(*ph[1:])
                elif ph[0] == "do":
                    if ph[2]:
                        ph[2](act, A, link)
                elif ph[0] == "mix":
                    mixers[ph[1]]["act"](act, A, link, ph)

        @block.vector
        def _(dve):
            V = nc.vector
            link = Chain(dve, s_dve)

            def ada(layer, c, dyn=None):
                a = 18 * layer + c
                n_w = 16 * (a // 2 + 1)
                dve.wait_ge(s_adaw[a % 2], n_w if dyn is None else dyn * 8 + n_w)
                if dyn is not None:
                    dve.wait_ge(s_col, dyn + (a - 1))
                elif a >= 2:
                    dve.wait_ge(s_col, a - 1)
                for s in range(2 if layer == 0 else 1):
                    which = s if layer < 2 else 2
                    for k in range(DT):
                        sc = SC[:, which, k:k + 1]
                        if k == 0:
                            link(V.tensor_scalar(ACC[:, a % 2, s, :], ADAW[:, a % 2, k, :], sc, None, ALU.mult))
                        else:
                            ins = V.scalar_tensor_tensor(ACC[:, a % 2, s, :], ADAW[:, a % 2, k, :], sc,
                                                         ACC[:, a % 2, s, :], ALU.mult, ALU.add)
                            if k < DT - 1 or (layer == 0 and s == 0):
                                link(ins)
                ins.then_inc(s_acc, 1)

            def mods(layer, c0, c1, n):
                dve.wait_ge(s_col, 18 * layer + c1)
                bias = vec("ada_b", 72 * layer, 72) if layer < 2 else vec("mod_b_2", 72 * (layer - 2), 72)
                a, b = 4 * c0, 4 * c1
                if layer == 0:
                    link(V.tensor_tensor(MOD[:, 4, a:b], ADA_PS[:, 128 + a:128 + b], bias[:, a:b], ALU.add))
                V.tensor_tensor(MOD[:, layer, a:b], ADA_PS[:, a:b], bias[:, a:b], ALU.add).then_inc(s_mod, 1)
                dve.wait_ge(s_mod, n)

            def gates(layer, k, w, ctx_too):
                for s, m in ((0, layer), (1, 4))[:2 if ctx_too else 1]:
                    g = MOD[:, m, 8 * k:8 * k + 8]
                    if layer < 2:
                        link(V.tensor_scalar(HG[:, s, :], g, w, None, ALU.mult))
                    else:
                        link(V.tensor_scalar(HG[:, s, :], g, 1.0, w / ALPHA, ALU.add, ALU.mult))

            def ffn(sec):
                T, t0, per, k0 = sec["T"], sec["t0"], sec["per"], sec["silu0"]

                def hidden(q, u, dyn):
                    idx = t0 + per * u + (2 * q if per == 4 else q)
                    f = 2 * u + q
                    if dyn is None:
                        dve.wait_ge(s_silu, k0 + f + 1)
                        if per == 4:
                            dve.wait_ge(s_mm, idx + 2)
                        o = H[:, f, 0:T]
                    else:
                        dve.wait_ge(s_silu, dyn * 2 + (k0 + f + 1))
                        if per == 4:
                            dve.wait_ge(s_mm, dyn * per + (idx + 2))
                        o = region(0, [FT * 2 * S])[:, bass.ds(dyn * (4 * S) + f * 2 * S, T)]
                    up = PS[(idx + 1) % 4][:, :] if per == 4 else PS[idx % 4][:, S:2 * S]
                    V.tensor_tensor(o, SIL[:, q, 0:T], up, ALU.mult).then_inc(s_ev, per // 2)

                def unit(u, dyn, with_ada):
                    for q in range(2):
                        if with_ada:
                            layer, first, _ = sec["ada"]
                            ada(layer, first + 2 * u + q, None if dyn is None else dyn * 2)
                        hidden(q, u, dyn)

                links = (16 - 1 if sec["ada"] and sec["ada"][0] == 0 else 7) * 2
                units_ada = sec["ada"][2] // 2 if sec["ada"] else 0
                pairs = units_ada // 2
                if pairs:
                    with steps(dve, 0, 2 * pairs, 2) as j:
                        link.loop(j, links, 2, pairs)
                        for u in range(2):
                            unit(u, j, True)
                        link.end()
                rest = 2 * pairs
                if units_ada % 2:
                    unit(rest, None, True)
                    rest += 1
                more = (PAIRS - rest) // 2
                if more:
                    with steps(dve, 0, 2 * more, 2) as j:
                        for u in range(2):
                            unit(rest + u, j, False)
                    rest += 2 * more
                if rest < PAIRS:
                    unit(rest, None, False)
                if sec is F[0]:
                    mods(0, 4, ADA_CHUNKS, 2)
                    gates(0, 2, 0.5, True)
                td = t0 + per * PAIRS
                xf = X[:, :, :, :].rearrange("p s k n -> p s (k n)")
                with steps(dve, 0, 4, 2) as j:
                    for u in range(2):
                        for q in range(2):
                            idx = td + 2 * u + q
                            n = 2 * u + q
                            dve.wait_ge(s_mm, j * 2 + (idx + 1))
                            for s in range(T // S):
                                xs = xf[:, s, bass.ds(j * (2 * S) + n * S, S)]
                                ins = V.scalar_tensor_tensor(xs, PS[idx % 4][:, s * S:(s + 1) * S],
                                                             HG[:, s, bass.ds(j * 2 + n, 1)], xs, ALU.mult, ALU.add)
                            ins.then_inc(s_ev, 1)
                dve.wait_ge(s_ev, sec["t1"])

            def rms(layer, k, T, n_rs, g, n_y):
                seqs = T // S
                for s, m in ((0, layer), (1, 4))[:seqs]:
                    link(V.scalar_tensor_tensor(GS[:, s, :], MOD[:, m, 8 * (k + 1):8 * (k + 2)], 1.0, g, ALU.add,
                                                ALU.mult))
                dve.wait_ge(s_rs, n_rs)
                link(V.reciprocal(RS[:, 0:T], RS[:, 0:T]))
                kt = DT // PIECES
                for i in range(0, DT, kt):
                    for s in range(seqs):
                        link(V.tensor_tensor(Y[:, i:i + kt, s * S:(s + 1) * S], X[:, s, i:i + kt],
                                             RS[:, s * S:(s + 1) * S].unsqueeze(1).to_broadcast([P, kt, S]),
                                             ALU.mult))
                    for s, m in ((0, layer), (1, 4))[:seqs]:
                        for j in range(i, i + kt):
                            y = Y[:, j, s * S:(s + 1) * S]
                            ins = V.tensor_scalar(y, y, GS[:, s, j:j + 1], MOD[:, m, 8 * k + j:8 * k + j + 1],
                                                  ALU.mult, ALU.add)
                    ins.then_inc(s_y, 1)
                dve.wait_ge(s_y, n_y)

            def scaled(n_rs, g, n_x):
                dve.wait_ge(s_rs, n_rs)
                link(V.reciprocal(RS[:, 0:S], RS[:, 0:S]))
                link(V.tensor_tensor(X[:, 0], X[:, 0], RS[:, 0:S].unsqueeze(1).to_broadcast([P, DT, S]), ALU.mult))
                for i in range(DT):
                    ins = V.tensor_scalar(X[:, 0, i], X[:, 0, i], g[:, i:i + 1], None, ALU.mult)
                ins.then_inc(s_xr, 1)
                dve.wait_ge(s_xr, n_x)

            def scale_of(layer, k):
                link(V.tensor_scalar(GS[:, 0, :], MOD[:, layer, 8 * (k + 1):8 * (k + 2)], 1.0, None, ALU.add))

            def modulate_piece(layer, k, i):
                for j in range(i, i + DT // PIECES):
                    ins = V.tensor_scalar(Y[:, j, 0:S], X[:, 0, j], GS[:, 0, j:j + 1],
                                          MOD[:, layer, 8 * k + j:8 * k + j + 1], ALU.mult, ALU.add)
                ins.then_inc(s_y, 1)

            def modulate(layer, k, n_y):
                scale_of(layer, k)
                for i in range(0, DT, DT // PIECES):
                    modulate_piece(layer, k, i)
                dve.wait_ge(s_y, n_y)

            def center(n_ns, n_x):
                dve.wait_ge(s_ns, n_ns)
                link(V.tensor_scalar(RS[:, 0:S], NORM_PS[:, 0:S], 1.0 / D, None, ALU.mult))
                kt = DT // PIECES
                for i in range(PIECES):
                    x = X[:, 0, kt * i:kt * (i + 1)]
                    V.tensor_tensor(x, x, RS[:, 0:S].unsqueeze(1).to_broadcast([P, kt, S]),
                                    ALU.subtract).then_inc(s_xr, 1)
                dve.wait_ge(s_xr, n_x)

            def layer_norm(n_rs, at, n_x, then, n_y):
                if then:
                    scale_of(*then)
                dve.wait_ge(s_rs, n_rs)
                link(V.reciprocal(RS[:, 0:S], RS[:, 0:S]))
                kt = DT // PIECES
                for i in range(0, DT, kt):
                    x = X[:, 0, i:i + kt]
                    link(V.tensor_tensor(x, x, RS[:, 0:S].unsqueeze(1).to_broadcast([P, kt, S]), ALU.mult))
                    for j in range(i, i + kt):
                        ins = V.tensor_scalar(X[:, 0, j], X[:, 0, j], vec("ln_g_2", at + j), vec("ln_b_2", at + j),
                                              ALU.mult, ALU.add)
                    if i + kt < DT:
                        link(ins)
                    else:
                        ins.then_inc(s_xr, 1)
                        dve.wait_ge(s_xr, n_x)
                    if then:
                        modulate_piece(*then, i)
                if then:
                    dve.wait_ge(s_y, n_y)

            for v in range(0, VEC_TILES, 4):
                m = min(4, VEC_TILES - v)
                dve.wait_ge(s_mm, v + m)
                V.tensor_copy(VEC[:, v * P:min((v + m) * P, VEC_ROWS)],
                              PS[v // 4][:, 0:min(m * P, VEC_ROWS - v * P)]).then_inc(s_ev, m)
            dve.wait_ge(s_ev, VEC_TILES)
            dve.wait_ge(s_sc, 1)
            for c in range(4):
                ada(0, c)
            mods(0, 0, 4, 1)
            for s in range(2):
                for k in range(DT):
                    dve.wait_ge(s_xT, 8 * s + k + 1)
                    V.tensor_copy(X[:, s, k, :], PS[6 + k % 2][:, 0:S]).then_inc(s_xc, 1)
            dve.wait_ge(s_xc, 16)
            for ph in phases:
                kind, args = ph[0], ph[1:]
                if kind == "ffn":
                    ffn(F[args[0]])
                elif kind == "do":
                    if ph[3]:
                        ph[3](dve, V, link)
                elif kind == "mix":
                    mixers[args[0]]["dve"](dve, V, link, ph)
                elif kind in ("mods", "gates", "rms", "scaled", "modulate", "center", "layer_norm"):
                    dict(mods=mods, gates=gates, rms=rms, scaled=scaled, modulate=modulate, center=center,
                         layer_norm=layer_norm)[kind](*args)
            for h in range(2):
                for g in range(2):
                    dve.wait_ge(s_o, 2 * h + g + 1)
                    V.tensor_copy(OUT[:, h, g * 512:(g + 1) * 512], PS[g][:, :]).then_inc(s_oc, 1)


INPUTS = ["x", "ctx", "ada_w", "ffn1_w_gu", "ffn1_w_down", "ffn2_w_gu", "ffn2_w_down", "mod_w_2", "ffn_in_2", "ffn_out_2",
          "e_w_in", "e_w_up", "e_a_up", "e_g_up", "e_w_out", "o_w_in", "o_pool_w", "o_w_out", "positions_2",
          "even_w_in_2", "rg_wa_2", "rg_wx_2", "gla_wa2_2", "even_w_out_2", "odd_w_in_2", "w_q_up_2", "w_kv_up_2",
          "odd_w_out_2"]


def kernel(**inputs):
    import concourse.bacc as bacc
    from concourse.bass_utils import run_bass_kernel_spmd

    nc = bacc.Bacc("TRN2", target_bir_lowering=False, num_devices=1)
    table, table_at = constant_table()
    arrays, t = {}, {}
    for name in INPUTS + [v for v, _ in VEC_LIST]:
        a = np.ascontiguousarray(inputs[name])
        arrays[f"in_{name}"] = a
        t[name] = nc.dram_tensor(f"in_{name}", a.shape, mybir.dt.from_np(a.dtype), kind="ExternalInput").ap()
    arrays["in_table"] = table
    t["table"] = nc.dram_tensor("in_table", table.shape, F32, kind="ExternalInput").ap()
    out = nc.dram_tensor("out_0", [S, D], F32, kind="ExternalOutput").ap()
    build(nc, t, out, table_at)
    r = run_bass_kernel_spmd(nc, [arrays], core_ids=[0])
    return np.asarray(r.results[0]["out_0"]).reshape(1, S, D)
```
